# Optimizing a Trainium2 kernel written in Bass

```python
import math
import jax, jax.numpy as jnp
from jax import lax
import numpy as np

D_MODEL = 1024
BATCH = 1
SEQ = 256
DEPTH = 2

D_FF = 2816
PLE_DIM = 256
EPS = 1e-6
Q_BLOCK = 128
A_HEADS = 16
A_DC = 128
A_DCQ = 256
IDX_HEADS = 8
IDX_DIM = 64
TOPK_MAX = 256
SSM_DINNER = 2 * D_MODEL
SSM_HEADDIM = 64
SSM_HEADS = SSM_DINNER // SSM_HEADDIM
SSM_GROUPS = 8
SSM_STATE = 128
SSM_CONV = 4
SSM_CHUNK = 128
SSM_CONV_DIM = SSM_DINNER + 2 * SSM_GROUPS * SSM_STATE
C_GROUPS = ((128, 1), (512, 4), (2048, 16))
C_HEADS = 8
C_HEADDIM = 64
C_COLS = len(C_GROUPS) * 3 * C_HEADS * C_HEADDIM
REL_BUCKETS = 32
REL_MAX_DIST = 2048
REL_HEADS = A_HEADS + len(C_GROUPS) * C_HEADS
IN_SPLIT_SIZES = (A_DCQ, A_DC, IDX_DIM, IDX_HEADS,
                  SSM_DINNER, SSM_CONV_DIM, SSM_HEADS,
                  C_COLS,
                  D_MODEL, D_MODEL, D_MODEL)
IN_COLS = sum(IN_SPLIT_SIZES)

kernel_name = 'hybrid_gated_dsa_ssd_dilated'

def rmsnorm(x, g):
    xf = x.astype(jnp.float32)
    y = xf * lax.rsqrt(jnp.mean(xf * xf, axis=-1, keepdims=True) + EPS)
    return (y * g.astype(jnp.float32)).astype(x.dtype)

def swiglu(h, w_gate, w_up, w_down):
    return (jax.nn.silu(h @ w_gate) * (h @ w_up)) @ w_down

def to_blocks(a, size=Q_BLOCK):
    a = a.reshape(a.shape[0], a.shape[1] // size, size, *a.shape[2:])
    return jnp.swapaxes(a, 0, 1)

def from_blocks(a):
    a = jnp.swapaxes(a, 0, 1)
    return a.reshape(a.shape[0], a.shape[1] * a.shape[2], *a.shape[3:])

def rel_bucket(dist):
    max_exact = REL_BUCKETS // 2
    d = jnp.maximum(dist, 0)
    df = jnp.maximum(d, 1).astype(jnp.float32)
    large = max_exact + (jnp.log(df / max_exact) / math.log(REL_MAX_DIST / max_exact)
                         * (REL_BUCKETS - max_exact)).astype(jnp.int32)
    large = jnp.minimum(large, REL_BUCKETS - 1)
    return jnp.where(d < max_exact, d, large)

def dsa_mixer(cq, ckv, k_idx, w_idx, cq_norm, ckv_norm, w_uq, w_iq, bias_tbl):
    bsz, t, _ = cq.shape
    topk = min(TOPK_MAX, t // 4)
    cqn = rmsnorm(cq, cq_norm)
    q_lat = (cqn @ w_uq).reshape(bsz, t, A_HEADS, A_DC)
    q_idx = (cqn @ w_iq).reshape(bsz, t, IDX_HEADS, IDX_DIM)
    kv = rmsnorm(ckv, ckv_norm)
    w_idx = w_idx * (IDX_HEADS * IDX_DIM) ** -0.5
    key_pos = jnp.arange(t)
    tbl = bias_tbl[:, :A_HEADS]
    scale = A_DC ** -0.5

    def block(args):
        qb, qib, wb, pos = args
        rel = jax.nn.relu(jnp.einsum('bqhd,bsd->bqhs', qib, k_idx))
        score = jnp.einsum('bqhs,bqh->bqs', rel, wb).astype(jnp.float32)
        causal = key_pos[None, :] <= pos[:, None]
        score = jnp.where(causal[None], score, -jnp.inf)
        _, sel = lax.top_k(score, topk)
        kv_sel = jax.vmap(lambda c, i: c[i])(kv, sel)
        dist = pos[None, :, None] - sel
        bias = jnp.swapaxes(tbl[rel_bucket(dist)], -1, -2).astype(jnp.float32)
        logits = jnp.einsum('bqhd,bqkd->bqhk', qb, kv_sel).astype(jnp.float32) * scale + bias
        logits = jnp.where((dist >= 0)[:, :, None, :], logits, -jnp.inf)
        probs = jax.nn.softmax(logits, axis=-1).astype(kv_sel.dtype)
        return jnp.einsum('bqhk,bqkd->bqhd', probs, kv_sel)

    out = lax.map(block, (to_blocks(q_lat), to_blocks(q_idx), to_blocks(w_idx),
                          key_pos.reshape(-1, Q_BLOCK)))
    return from_blocks(out).reshape(bsz, t, A_HEADS * A_DC)

def ssd_mixer(z, xbc, dt_raw, conv_w, conv_b, dt_bias, a_log, d_skip, norm_g):
    bsz, t, _ = xbc.shape
    G, HG, P, N = SSM_GROUPS, SSM_HEADS // SSM_GROUPS, SSM_HEADDIM, SSM_STATE
    conv = lax.conv_general_dilated(xbc, conv_w, window_strides=(1,),
                                    padding=[(SSM_CONV - 1, 0)],
                                    dimension_numbers=('NWC', 'WIO', 'NWC'),
                                    feature_group_count=SSM_CONV_DIM)
    xbc = jax.nn.silu(conv + conv_b)
    xs, bm, cm = jnp.split(xbc, [SSM_DINNER, SSM_DINNER + G * N], axis=-1)
    xs = xs.reshape(bsz, t, G, HG, P).astype(jnp.float32)
    bm = bm.reshape(bsz, t, G, N).astype(jnp.float32)
    cm = cm.reshape(bsz, t, G, N).astype(jnp.float32)
    dt = jax.nn.softplus(dt_raw.astype(jnp.float32) + dt_bias.astype(jnp.float32)).reshape(bsz, t, G, HG)
    a = -jnp.exp(a_log.astype(jnp.float32)).reshape(G, HG)
    tril = jnp.tril(jnp.ones((SSM_CHUNK, SSM_CHUNK), dtype=bool))[None, :, :, None, None]

    def step(state, inp):
        xc, bc, cc, dtc = inp
        cum = jnp.cumsum(dtc * a, axis=1)
        seg = cum[:, :, None] - cum[:, None, :]
        decay = jnp.exp(jnp.where(tril, seg, -jnp.inf))
        cb = jnp.einsum('bign,bjgn->bijg', cc, bc)
        wgt = decay * cb[..., None] * dtc[:, None]
        y_diag = jnp.einsum('bijgh,bjghp->bighp', wgt, xc)
        y_off = jnp.einsum('bign,bghpn->bighp', cc, state) * jnp.exp(cum)[..., None]
        last = cum[:, -1]
        w_state = jnp.exp(last[:, None] - cum) * dtc
        new_state = (state * jnp.exp(last)[..., None, None]
                     + jnp.einsum('bjgh,bjghp,bjgn->bghpn', w_state, xc, bc))
        return new_state, y_diag + y_off

    state0 = jnp.zeros((bsz, G, HG, P, N), jnp.float32)
    _, ys = lax.scan(step, state0, (to_blocks(xs, SSM_CHUNK), to_blocks(bm, SSM_CHUNK),
                                    to_blocks(cm, SSM_CHUNK), to_blocks(dt, SSM_CHUNK)))
    y = from_blocks(ys) + xs * d_skip.astype(jnp.float32).reshape(G, HG)[:, :, None]
    y = y * jax.nn.silu(z.astype(jnp.float32)).reshape(bsz, t, G, HG, P)
    y = y.reshape(bsz, t, G, HG * P)
    y = y * lax.rsqrt(jnp.mean(y * y, axis=-1, keepdims=True) + EPS)
    y = y.reshape(bsz, t, SSM_DINNER) * norm_g.astype(jnp.float32)
    return y.astype(z.dtype)

def dilated_mixer(qkv, bias_tbl):
    bsz, t, _ = qkv.shape
    qkv = qkv.reshape(bsz, t, len(C_GROUPS), 3, C_HEADS, C_HEADDIM)
    q_pos = jnp.arange(t).reshape(-1, Q_BLOCK)
    scale = C_HEADDIM ** -0.5
    outs, lses = [], []
    for g, (window, dilation) in enumerate(C_GROUPS):
        q, k, v = qkv[:, :, g, 0], qkv[:, :, g, 1], qkv[:, :, g, 2]
        offs = jnp.arange(window // dilation + 1) * dilation
        tbl = bias_tbl[:, A_HEADS + g * C_HEADS:A_HEADS + (g + 1) * C_HEADS]
        bias = tbl[rel_bucket(offs)].T.astype(jnp.float32)

        def block(args, k=k, v=v, offs=offs, bias=bias):
            qb, pos = args
            idx = pos[:, None] - offs[None, :]
            valid = idx >= 0
            idx = jnp.maximum(idx, 0)
            kb = k[:, idx]
            vb = v[:, idx]
            logits = jnp.einsum('bqhd,bqkhd->bqhk', qb, kb).astype(jnp.float32) * scale + bias
            logits = jnp.where(valid[None, :, None, :], logits, -jnp.inf)
            lse = jax.nn.logsumexp(logits, axis=-1)
            probs = jnp.exp(logits - lse[..., None]).astype(vb.dtype)
            return jnp.einsum('bqhk,bqkhd->bqhd', probs, vb), lse

        o, lse = lax.map(block, (to_blocks(q), q_pos))
        outs.append(from_blocks(o))
        lses.append(from_blocks(lse))
    wts = jax.nn.softmax(jnp.stack(lses), axis=0)
    out = jnp.einsum('gbth,gbthd->bthd', wts.astype(qkv.dtype), jnp.stack(outs))
    return out.reshape(bsz, t, C_HEADS * C_HEADDIM)

def setup_inputs(seed: int = 0) -> dict:
    key = jax.random.key(seed)
    ks = iter(jax.random.split(key, 48))
    f32 = jnp.float32
    L = DEPTH

    def nrm(shape, fan_in):
        return jax.random.normal(next(ks), shape, f32) * fan_in ** -0.5

    def gain(shape):
        return 1.0 + 0.05 * jax.random.normal(next(ks), shape, f32)

    def small(shape, s=0.02):
        return s * jax.random.normal(next(ks), shape, f32)

    dt0 = jnp.exp(jax.random.uniform(next(ks), (L, SSM_HEADS), f32, math.log(1e-3), math.log(1e-1)))
    return {
        'x': jax.random.normal(next(ks), (BATCH, SEQ, D_MODEL), f32),
        'p': jax.random.normal(next(ks), (DEPTH, BATCH, SEQ, PLE_DIM), f32),
        'rel_bias': 0.5 * jax.random.normal(next(ks), (REL_BUCKETS, REL_HEADS), f32),
        'final_norm': gain((D_MODEL,)),
        'ffn1_norm': gain((L, D_MODEL)),
        'ffn1_gate': nrm((L, D_MODEL, D_FF), D_MODEL),
        'ffn1_up': nrm((L, D_MODEL, D_FF), D_MODEL),
        'ffn1_down': nrm((L, D_FF, D_MODEL), D_FF),
        'mix_norm': gain((L, D_MODEL)),
        'w_in': nrm((L, D_MODEL, IN_COLS), D_MODEL),
        'cq_norm': gain((L, A_DCQ)),
        'ckv_norm': gain((L, A_DC)),
        'w_uq': nrm((L, A_DCQ, A_HEADS * A_DC), A_DCQ),
        'w_iq': nrm((L, A_DCQ, IDX_HEADS * IDX_DIM), A_DCQ),
        'conv_w': nrm((L, SSM_CONV, 1, SSM_CONV_DIM), SSM_CONV),
        'conv_b': small((L, SSM_CONV_DIM)),
        'dt_bias': dt0 + jnp.log(-jnp.expm1(-dt0)),
        'a_log': jnp.log(jax.random.uniform(next(ks), (L, SSM_HEADS), f32, 1.0, 16.0)),
        'd_skip': gain((L, SSM_HEADS)),
        'ssm_norm': gain((L, SSM_DINNER)),
        'w_out_a': nrm((L, A_HEADS * A_DC, D_MODEL), A_HEADS * A_DC),
        'w_out_b': nrm((L, SSM_DINNER, D_MODEL), SSM_DINNER),
        'w_out_c': nrm((L, C_HEADS * C_HEADDIM, D_MODEL), C_HEADS * C_HEADDIM),
        'w_o': nrm((L, D_MODEL, D_MODEL), D_MODEL),
        'ffn2_norm': gain((L, D_MODEL)),
        'ffn2_gate': nrm((L, D_MODEL, D_FF), D_MODEL),
        'ffn2_up': nrm((L, D_MODEL, D_FF), D_MODEL),
        'ffn2_down': nrm((L, D_FF, D_MODEL), D_FF),
        'ple_norm': gain((L, D_MODEL)),
        'w_ple_gate': nrm((L, D_MODEL, D_MODEL), D_MODEL),
        'w_ple_proj': nrm((L, PLE_DIM, D_MODEL), PLE_DIM),
    }

def reference(x, p, rel_bias, final_norm,
              ffn1_norm, ffn1_gate, ffn1_up, ffn1_down,
              mix_norm, w_in, cq_norm, ckv_norm, w_uq, w_iq,
              conv_w, conv_b, dt_bias, a_log, d_skip, ssm_norm,
              w_out_a, w_out_b, w_out_c, w_o,
              ffn2_norm, ffn2_gate, ffn2_up, ffn2_down,
              ple_norm, w_ple_gate, w_ple_proj):
    split_at = np.cumsum(IN_SPLIT_SIZES)[:-1].tolist()
    for i in range(DEPTH):
        h = rmsnorm(x, ffn1_norm[i])
        x = x + 0.5 * swiglu(h, ffn1_gate[i], ffn1_up[i], ffn1_down[i])
        h = rmsnorm(x, mix_norm[i])
        (cq, ckv, k_idx, w_idx, z, xbc, dt_raw, qkv_c,
         g_a, g_b, g_c) = jnp.split(h @ w_in[i], split_at, axis=-1)
        y_a = dsa_mixer(cq, ckv, k_idx, w_idx, cq_norm[i], ckv_norm[i], w_uq[i], w_iq[i], rel_bias) @ w_out_a[i]
        y_b = ssd_mixer(z, xbc, dt_raw, conv_w[i], conv_b[i], dt_bias[i], a_log[i], d_skip[i], ssm_norm[i]) @ w_out_b[i]
        y_c = dilated_mixer(qkv_c, rel_bias) @ w_out_c[i]
        merged = jax.nn.sigmoid(g_a) * y_a + jax.nn.sigmoid(g_b) * y_b + jax.nn.sigmoid(g_c) * y_c
        x = x + merged @ w_o[i]
        h = rmsnorm(x, ffn2_norm[i])
        x = x + 0.5 * swiglu(h, ffn2_gate[i], ffn2_up[i], ffn2_down[i])
        h = rmsnorm(x, ple_norm[i])
        x = x + jax.nn.sigmoid(h @ w_ple_gate[i]) * (p[i] @ w_ple_proj[i])
    return rmsnorm(x, final_norm)


_drawn_inputs = setup_inputs


def setup_inputs(seed=0):
    import zlib

    import numpy as np

    out = dict(_drawn_inputs(seed))
    spreads = {}
    factors = {'ckv_norm': 4.468, 'conv_b': 3.054, 'd_skip': 2.807, 'ple_norm': 4.366}
    for name, (base, spread) in spreads.items():
        noise = np.random.default_rng([zlib.crc32(name.encode()), seed]).standard_normal(out[name].shape)
        drawn = base * np.exp(spread * noise) if base else spread * noise
        out[name] = __import__('jax').numpy.asarray(drawn.astype(out[name].dtype))
    for name, factor in factors.items():
        out[name] = (out[name] * factor).astype(out[name].dtype)
    return out
```

```python
import math
from contextlib import ExitStack

import numpy as np
import concourse.bass as bass
from concourse import mybir

D_MODEL, SEQ, DEPTH, D_FF, PLE_DIM, EPS = 1024, 256, 2, 2816, 256, 1e-6
P = 128
TOK = SEQ // P
KD = D_MODEL // P
A_HEADS, A_DC, A_DCQ = 16, 128, 256
IDX_HEADS, IDX_DIM = 8, 64
TOPK = min(256, SEQ // 4)
GROUPS, HG, HEADDIM, STATE = 8, 4, 64, 128
CG, C_HEADS, C_DIM = 3, 8, 64
DILATED = ((128, 1), (512, 4), (2048, 16))
BUCKETS, MAX_DIST = 32, 2048
HEADS = A_HEADS + CG * C_HEADS
SSM = GROUPS * HG * HEADDIM
TW = 1024
SLOTS = 6
AHEAD = 4
MASKED = -1.0e30
SCORE_MASK, SCORE_TAKEN, SCORE_CUT = -3.0e38, -3.3e38, -3.2e38
DIST = 3 * P - 1
ROW = 384
PAIRS = D_FF // (2 * P)
AC_STEPS = 4

_SIZES = (A_DCQ, A_DC, IDX_DIM, IDX_HEADS, SSM, SSM + 2 * GROUPS * STATE, GROUPS * HG,
          CG * 3 * C_HEADS * C_DIM, D_MODEL, D_MODEL, D_MODEL)
C_CQ, C_CKV, C_KI, C_WI, C_Z, C_XBC, C_DT, C_QKV, C_GA, C_GB, C_GC = (
    int(v) for v in np.concatenate([[0], np.cumsum(_SIZES)[:-1]]))

G_NORM = 0
G_CQ = 32
G_CKV = 34
G_EXPA = 35
G_DTB = 67
G_GRP = 99
GRP = 26
NPRM = G_GRP + GROUPS * GRP

SEGMENTS = [
    ("f1pre", 1, 4), ("f1loop", PAIRS - 1, 6), ("f1tail", 1, 2),
    ("m0", 1, 31), ("bloop", GROUPS - 1, 8), ("btail", 1, 2),
    ("ac", AC_STEPS, 15), ("out", 1, 12),
    ("f2pre", 1, 4), ("f2loop", PAIRS - 1, 6), ("f2tail", 1, 2),
    ("ple", 1, 10),
]


SLOT_PATTERN = {6: (0, 1, 2, 3, 4, 5), 8: (0, 1, 2, 3, 4, 5, 2, 3),
                15: (0, 1, 2, 3, 4, 0, 1, 2, 5, 3, 0, 1, 2, 4, 5)}


def close_ring(slots, total):
    if len(slots) == total:
        return slots if all(slots[k] not in slots[k - AHEAD + 1:] for k in range(AHEAD - 1)) else None
    recent = list(dict.fromkeys(reversed(slots)))
    for s in recent[::-1]:
        if s not in slots[len(slots) - AHEAD + 1:]:
            found = close_ring(slots + [s], total)
            if found:
                return found
    return None


def plan_tiles():
    seq, seg_at, pattern = [], {}, {}
    owed = []
    for name, reps, n in SEGMENTS:
        lead = owed
        recent = list(dict.fromkeys(s for _, s in reversed(seq)))
        lru = [s for s in range(SLOTS) if s not in recent] + recent[::-1]
        if reps > 1:
            order = lead + [s for s in lru if s not in lead] if lead else lru
            pat = [order[k] for k in SLOT_PATTERN[n]]
            assert len(pat) == n
            pattern[name] = pat
        seg_at[name] = len(seq)
        for r in range(reps):
            for k in range(n):
                if reps > 1:
                    s = pattern[name][k]
                elif k < len(lead):
                    s = lead[k]
                else:
                    recent = list(dict.fromkeys(s for _, s in reversed(seq)))
                    s = ([s for s in range(SLOTS) if s not in recent] + recent[::-1])[0]
                seq.append((name, s))
        owed = pattern[name][:AHEAD] if reps > 1 else owed[n:]
    slots = [s for _, s in seq]
    total = len(slots)
    slots = close_ring(slots[:seg_at[SEGMENTS[-1][0]]], total)
    twice = slots + slots
    back = []
    for t in range(total, 2 * total):
        d = next(d for d in range(1, 2 * total) if twice[t - d] == twice[t])
        assert d >= AHEAD, (seq[t - total][0], t - total, d)
        back.append(min(d, SLOTS))
    count = [slots[:t].count(slots[t]) for t in range(total)]
    return slots, seg_at, back, count, total


SLOT_OF, SEG_AT, BACK, COUNT, TILES = plan_tiles()
USES = [SLOT_OF.count(s) for s in range(SLOTS)]
SEG_N = {name: (reps, n) for name, reps, n in SEGMENTS}


def tile_numbers(seg, pos, it, layer):
    reps, n = SEG_N[seg]
    t0 = SEG_AT[seg] + pos
    if reps == 1:
        return layer * TILES + t0, SLOT_OF[t0], layer * USES[SLOT_OF[t0]] + COUNT[t0], BACK[t0]
    every = [t0 + n * r for r in range(reps)]
    assert len({SLOT_OF[t] for t in every}) == 1
    s = SLOT_OF[t0]
    step = COUNT[t0 + n] - COUNT[t0]
    assert all(COUNT[t] == COUNT[t0] + step * r for r, t in enumerate(every))
    return (layer * TILES + (it * n + t0), s, layer * USES[s] + (it * step + COUNT[t0]),
            min(BACK[t] for t in every))


def _norm(r):
    return (1, [(b, f"norm{r}") for b in ("W0", "W1", "S0", "S1")])


def _ffn(f):
    return [(PAIRS, [("W0", f"{f}even"), ("W1", f"{f}odd")])]


FILL_ORDER = (
    [_norm(0)] + _ffn("f1") + [_norm(1)]
    + [(1, [("W0", "small0"), ("W1", "small1")]),
       (3, [("W0", "v_even"), ("W1", "v_odd")]),
       (1, [("S0", "cqT"), ("S1", "kvT"), ("S0", "cum")]),
       (2, [("W0", "gb_even"), ("W1", "gb_odd")]),
       (1, [("S0", "qi0"), ("S1", "qi1")]),
       (1, [("W0", "x_first"), ("W1", "bc_first"), ("W0", "z_first")]),
       (2, [("S0", "sc1_even"), ("S1", "sc1_odd")]),
       (1, [("S0", "sc0_even"), ("S1", "sc0_odd")]),
       (GROUPS - 1, [("W0", "seg0"), ("W1", "seg1"), ("S0", "xT"), ("S1", "bcb"), ("W0", "x"),
                     ("S1", "state"), ("S0", "ydiag"), ("S1", "yoff"), ("W1", "bc"),
                     ("S1", "yT"), ("W0", "z")]),
       (1, [("W0", "seg0_last"), ("W1", "seg1_last"), ("S0", "xT_last"), ("S1", "bcb_last"),
            ("S1", "state_last"), ("S0", "ydiag_last"), ("S1", "yoff_last"), ("S1", "yT_last")]),
       (AC_STEPS, [("W0", "qa0"), ("W1", "qa1"), ("W0", "qk0"), ("S0", "la0"), ("S1", "la1"),
                   ("W1", "qk1"), ("S0", "la2"), ("W0", "qk2"),
                   ("S0", "lc0"), ("S1", "lc1"), ("S0", "lc2"), ("S1", "lc3"), ("S0", "lc4"),
                   ("S1", "lc5"), ("W1", "ga"), ("S1", "pa0"), ("S0", "pa1"), ("S1", "pa2"),
                   ("W0", "gc"), ("S0", "oa0"), ("S1", "oa1"),
                   ("S0", "pc0"), ("S1", "pc1"), ("S0", "pc2"), ("S1", "pc3"), ("S0", "pc4"),
                   ("S1", "oc"), ("S0", "ocT")]),
       (1, [("W0", "mT"), ("W1", "mT"), ("S0", "mT"), ("S1", "mT")])]
    + [_norm(2)] + _ffn("f2") + [_norm(3)]
    + [(1, [("W0", "pg"), ("W1", "pg"), ("S0", "pg"), ("S1", "pg")])]
)


BY_TILES = {"qi1", "qa1", "f1even", "f1odd", "f2even", "f2odd", "small0", "small1", "v_even", "v_odd", "gb_even", "gb_odd",
            "x_first", "bc_first", "z_first", "x", "bc", "z", "qk0", "qk1", "qk2", "ga", "gc", "pg"}


def plan_fills(without=()):
    at, step, total = {}, {}, dict.fromkeys(("W0", "W1", "S0", "S1"), 0)
    for reps, fills in FILL_ORDER:
        fills = [f for f in fills if f[1] not in without]
        per = {b: sum(1 for x, _ in fills if x == b) for b in total}
        seen = dict.fromkeys(total, 0)
        for b, name in fills:
            at[b, name] = total[b] + seen[b]
            step[b, name] = per[b]
            seen[b] += 1
        for b in total:
            total[b] += per[b] * reps
    return at, step, total


FREE_PLAN, FULL_PLAN = plan_fills(), plan_fills(BY_TILES)

ACC_USES = {"f1": 0, "b": 1, "a": 2, "c": 3, "o": 4, "f2": 5, "ple": 6}
Y_AT = {"f1": 0, "b": PAIRS, "a": PAIRS + GROUPS, "c": PAIRS + GROUPS + AC_STEPS,
        "f2": PAIRS + GROUPS + AC_STEPS + 1}
Y_USES = 2 * PAIRS + GROUPS + AC_STEPS + 1

PER_LAYER = dict(
    x_done=4, squares=4, rstd=4, xn=4, gained=20, h_hi=20, h_lo=20,
    ffn_tanh=4 * PAIRS, y_src=Y_USES, y_hi=Y_USES, y_lo=Y_USES, 
    acc_free=7,
    small=2, prep_squares=1, prep_rstd=1, prep_n=1, cq_gained=1, cq_hi=2, cq_lo=2, ki=1,
    kv=1, dt_in=1, dt_ln=1, da=1, ecum=1, wlast=1, v_sb=6, gates=8 + 4 + 4 + 4,
    qi=2, relu=6, weighted=6, chosen=1,
    dau=GROUPS, decay=2 * GROUPS, ssd_in=GROUPS, scan_w=GROUPS, state=GROUPS, y_sum=GROUPS,
    y_squares=GROUPS, y_rstd=GROUPS, yn=GROUPS, pre_x=GROUPS, pre_bc=GROUPS, conv=GROUPS,
    conv_tanh=GROUPS, xbc=GROUPS, z_tanh=GROUPS, zz=GROUPS, taps=GROUPS,
    qa=AC_STEPS, qk=3 * AC_STEPS, la=AC_STEPS, ea=AC_STEPS, na=AC_STEPS, pa=3 * AC_STEPS,
    lc=AC_STEPS, ec=AC_STEPS, nc_=AC_STEPS, pc=5 * AC_STEPS, oc=AC_STEPS,
    branch_a=1, merged=1,
)


SEEDED = ("x_done", "y_src", "acc_free", "conv", "y_sum", "pc", "lc")


def trunk(nc, x_in, weights, params, final_gain, ple_in, rel_bias, constants, one_hot, out):
    f32, f32r, bf16 = mybir.dt.float32, mybir.dt.float32r, mybir.dt.bfloat16
    ACT, ALU, AX = mybir.ActivationFunctionType, mybir.AluOpType, mybir.AxisListType
    MUL, ADD, SUB, MAX = ALU.mult, ALU.add, ALU.subtract, ALU.max

    with ExitStack() as ctx:
        def sb(name, shape, dt=f32):
            return ctx.enter_context(nc.sbuf_tensor(name, shape, dt))

        def sem(name):
            return ctx.enter_context(nc.semaphore(name))

        raw = [sb(f"raw{s}", [P, TW]) for s in range(SLOTS)]
        w_hi = [sb(f"w_hi{s}", [P, TW], f32r) for s in range(SLOTS)]
        w_lo = [sb(f"w_lo{s}", [P, TW], f32r) for s in range(SLOTS)]
        x = sb("x", [P, TOK, D_MODEL])
        h_hi = sb("h_hi", [P, KD, SEQ], f32r)
        h_lo = sb("h_lo", [P, KD, SEQ], f32r)
        y_hi = sb("y_hi", [P, 4, SEQ], f32r)
        y_lo = sb("y_lo", [P, 4, SEQ], f32r)
        c_hi = sb("c_hi", [P, 2, SEQ], f32r)
        c_lo = sb("c_lo", [P, 2, SEQ], f32r)
        ident = sb("ident", [P, P])
        upto = sb("upto", [P, P])
        after = sb("after", [P, P])
        causal = sb("causal", [P, 3 * P])
        zeros = sb("zeros", [P, 512], bf16)
        prm = sb("prm", [P, NPRM])
        minus_half = sb("minus_half", [P, 4])
        val = sb("val", [P, TOK, CG, 512])
        kvn = sb("kvn", [P, TOK, A_DC])
        kv_t = sb("kv_t", [P, SEQ])
        ki_t = sb("ki_t", [P, SEQ])
        score = sb("score", [P, 3 * P])
        top8 = sb("top8", [P, 2, 8])
        wix = sb("wix", [P, TOK, IDX_HEADS])
        dts = sb("dts", [P, TOK, 32])
        da = sb("da", [P, TOK, 32])
        wl = sb("wl", [P, 32])
        ecum = sb("ecum", [P, 32])
        gate_b = sb("gate_b", [P, TOK, D_MODEL])
        gate_a = sb("gate_a", [P, TOK, D_MODEL])
        gate_c = sb("gate_c", [P, TOK, D_MODEL])
        yc_t = sb("yc_t", [P, AC_STEPS, SEQ])
        bias = sb("bias", [P, 10, SEQ])
        stat = sb("stat", [P, 64])
        taps = sb("taps", [P, 20])
        arena = sb("arena", [P, 8192])
        biggest = [0]

        def part(at, shape, rows=P):
            n = int(np.prod(shape))
            biggest[0] = max(biggest[0], at + n)
            v = arena[0:rows, at:at + n]
            if len(shape) == 2:
                return v.rearrange("p (a b) -> p a b", a=shape[0])
            if len(shape) == 3:
                return v.rearrange("p (a b c) -> p a b c", a=shape[0], b=shape[1])
            return v

        xn = part(0, (TOK, D_MODEL))
        gained = part(2048, (4, 512))
        junk = part(4096, (1024,))
        act_f = part(5120, (2, SEQ))
        ffn_t = part(5632, (2, SEQ))
        small = part(0, (TOK, 512))
        cqn = part(1024, (TOK, A_DCQ))
        cqf = part(1536, (512,))
        dt_a = part(2048, (2, 64))
        relu = part(2304, (2, 512))
        qi = part(3328, (IDX_HEADS // 2, SEQ))
        ki2 = part(2304, (TOK, P))
        sq_m0 = part(5376, (256,))
        pre = part(5636, (4, 3 + SEQ))
        xbc = part(6672, (4, SEQ))
        conv_t = part(1024, (4, SEQ))
        dau = part(0, (TOK, 512))
        decay = part(1024, (TOK, 512))
        xdt = part(2048, (TOK, 256))
        xd = part(2560, (TOK, 256))
        xw = part(3072, (256,))
        b_tok = part(3328, (P,))
        cbm = part(3456, (TOK, P))
        zz = part(5120, (TOK, 256))
        ysum = part(3712, (TOK, 256))
        st = part(4224, (256,))
        yoffs = part(4480, (256,))
        sq_b = part(4736, (256,))
        yt_f = sb("yt_f", [P, 512])
        qa = part(0, (4, SEQ))
        la = part(1024, (4, 3 * P))
        pa = part(2560, (3, 512))
        pc = part(1024, (18, P))
        qk = part(4096, (CG, 2, SEQ))
        lc = part(5632, (2, CG, 3 * P))
        oc_f = part(7936, (TOK, P))
        mg = part(2048, (4, 512))
        pg = part(0, (TOK, D_MODEL))
        pin = part(2048, (512,))
        fgain = part(2048, (D_MODEL,))
        oh = part(0, (4, ROW), rows=33)
        tbl = part(1536, (HEADS,), rows=33)
        rb = part(1600, (4, ROW), rows=16)

        bank = {b: ctx.enter_context(nc.psum_tensor(f"bank_{b}", [P, 512], f32))
                for b in ("W0", "W1", "S0", "S1")}
        acc = [[ctx.enter_context(nc.psum_tensor(f"acc{t}{h}", [P, 512], f32)) for h in range(2)]
               for t in range(TOK)]
        W0, W1, S0, S1 = (bank[b] for b in ("W0", "W1", "S0", "S1"))
        arrived = [sem(f"arrived{s}") for s in range(SLOTS)]
        hi_done, lo_done, used = sem("hi_done"), sem("lo_done"), sem("used")
        full = {b: sem(f"full_{b}") for b in bank}
        free = {b: sem(f"free_{b}") for b in bank}
        ev = {n: sem(n) for n in PER_LAYER}
        x_loaded, consts_loaded, prm_loaded = sem("x_loaded"), sem("consts_loaded"), sem("prm_loaded")
        tbl_loaded, tables, tables_sb, tables_out = sem("tbl_loaded"), sem("tables"), sem("tables_sb"), sem("tables_out")
        bias_loaded, ple_loaded, fgain_loaded = sem("bias_loaded"), sem("ple_loaded"), sem("fgain_loaded")
        cleared, out_done, prm_halved, final = sem("cleared"), sem("out_done"), sem("prm_halved"), sem("final")

        scratch = nc.dram_tensor("distance_tables", (HEADS, ROW), f32, kind="Internal").ap()
        blocks = nc.dram_tensor("distance_blocks", (HEADS, P, SEQ), f32, kind="Internal").ap()
        blocks_out, pool_steps = sem("blocks_out"), sem("pool_steps")

        def ev_n(name, layer, n):
            return layer * PER_LAYER[name] + (n + (name in SEEDED))

        def free_n(b, name, layer, it=0):
            at, step, total = FREE_PLAN
            return layer * total[b] + (it * step[b, name] + (at[b, name] + 1))

        def fill_n(b, name, layer, it=0):
            at, step, total = FULL_PLAN
            return layer * total[b] + (it * step[b, name] + (at[b, name] + 1))

        def done(seg, pos, layer, it=0):
            return layer * TILES + (it * SEG_N[seg][1] + (SEG_AT[seg] + pos + 1 + SLOTS))

        def indexer_fill(k):
            if k < 4:
                first = 4 * (k // 2) + k % 2
                return (first, first + 2), SEQ, P, 1
            return tuple(range(k % 2, IDX_HEADS, 2)), P, 0, 0

        block = ctx.enter_context(nc.Block())

        @block.sync
        def _(sp):
            sp.dma_start(x[:, :, :], x_in.rearrange("o (t p) d -> p (o t) d", p=P)).then_inc(x_loaded, 16)
            sp.dma_start(ident[:, :], constants[:, 0:P]).then_inc(consts_loaded, 16)
            sp.dma_start(upto[:, :], constants[:, P:2 * P]).then_inc(consts_loaded, 16)
            sp.dma_start(after[:, :], constants[:, 2 * P:3 * P]).then_inc(consts_loaded, 16)
            sp.dma_start(causal[:, :], constants[:, 3 * P:6 * P]).then_inc(consts_loaded, 16)

            def stream(seg, layer, it=0):
                for pos in range(SEG_N[seg][1]):
                    t, s, count, back = tile_numbers(seg, pos, it, layer)
                    sp.wait_ge(lo_done, t - back + 1 + SLOTS)
                    sp.dma_start(raw[s][:, :], weights[bass.ts(t, 1), :, :].rearrange("o p n -> (o p) n")
                                 ).then_inc(arrived[s], 16)

            with sp.Fori(0, DEPTH) as layer:
                stream("f1pre", layer)
                for seg, reps, _ in SEGMENTS[1:]:
                    if reps > 1:
                        with sp.Fori(0, reps) as it:
                            stream(seg, layer, it)
                    else:
                        stream(seg, layer)

        @block.gpsimd
        def _(pool):
            pool.memset(minus_half[:, :], -0.5).then_inc(cleared, 1)
            pool.drain()
            pool.memset(zeros[:, :], 0.0).then_inc(cleared, 1)
            pool.drain()
            pool.memset(tbl[32:33, :], 1.0).then_inc(cleared, 1)
            pool.dma_start(tbl[0:32, :], rel_bias).then_inc(tbl_loaded, 16)
            pool.dma_start(oh, one_hot.rearrange("v r d -> r v d")).then_inc(tbl_loaded, 16)
            pool.wait_ge(tables_sb, 4)
            for v in range(4):
                first, n = (0, A_HEADS) if v == 0 else (A_HEADS + (v - 1) * C_HEADS, C_HEADS)
                pool.dma_start(scratch[first:first + n, :], rb[0:n, v, :]).then_inc(tables_out, 16)
            pool.wait_ge(tables_out, 64)
            for n in range(0, HEADS, HEADS // 4):
                skewed = bass.AP(tensor=scratch.tensor, offset=n * ROW + (P - 1),
                                 ap=[[ROW, HEADS // 4], [-1, P], [1, SEQ]])
                pool.dma_start(blocks[n:n + HEADS // 4, :, :], skewed).then_inc(blocks_out, 16)

            def row_power(mean, n_cols, scales, first):
                at = first
                for cols, scale in scales:
                    pool.tensor_scalar(stat[:, at:at + cols], stat[:, at:at + cols], scale, EPS, MUL, ADD)
                    at += cols
                    pool.drain()
                return pool.tensor_tensor(stat[:, first:first + n_cols], stat[:, first:first + n_cols],
                                          minus_half[:, 0:n_cols], ALU.pow)

            def settled():
                pool.sem_inc(pool_steps, 1)

            def norm(r, layer):
                pool.wait_ge(ev["squares"], ev_n("squares", layer, r + 1))
                settled()
                row_power(None, TOK, [(TOK, 1.0 / D_MODEL)], 0).then_inc(ev["rstd"], 1)
                pool.drain()

            def load_bias(layer, it):
                pool.wait_ge(blocks_out, 64)
                pool.wait_ge(ev["lc"], ev_n("lc", layer, it))
                settled()
                pool.dma_start(bias[:, 0:4, :], blocks[bass.ds(it * 4, 4), :, :].rearrange("h p s -> p h s")
                               ).then_inc(bias_loaded, 16)
                for g in range(CG):
                    heads = blocks[bass.ds(it * 2 + (A_HEADS + g * C_HEADS), 2), :, :]
                    pool.dma_start(bias[:, 4 + 2 * g:6 + 2 * g, :], heads.rearrange("h p s -> p h s")
                                   ).then_inc(bias_loaded, 16)

            def cum_steps(layer, g):
                for t in range(TOK):
                    pool.drain()
                    pool.tensor_tensor(
                        dau[:, t, :].rearrange("p (h i) -> p h i", h=HG),
                        upto[:, :].unsqueeze(1).broadcast_to([P, HG, P]),
                        da[:, t, bass.ts(g, HG)].unsqueeze(2).broadcast_to([P, HG, P]), MUL)
                pool.drain().then_inc(ev["dau"], 1)

            with pool.Fori(0, DEPTH) as layer:
                pool.wait_ge(ev["x_done"], ev_n("x_done", layer, 0))
                settled()
                pool.dma_start(prm[:, :], params[bass.ts(layer, 1), :, :].rearrange("o p n -> (o p) n")
                               ).then_inc(prm_loaded, 16)
                norm(0, layer)
                norm(1, layer)
                pool.wait_ge(ev["prep_squares"], ev_n("prep_squares", layer, 1))
                settled()
                row_power(None, 4, [(2, 1.0 / A_DCQ), (2, 1.0 / A_DC)], 4).then_inc(ev["prep_rstd"], 1)
                pool.wait_ge(full["S1"], fill_n("S1", "kvT", layer))
                pool.wait_ge(ev["da"], ev_n("da", layer, 1))
                settled()

                def group_taps(g):
                    pool.wait_ge(ev["conv"], ev_n("conv", layer, g))
                    settled()
                    pool.tensor_copy(taps[:, :], prm[:, bass.ds(g * GRP + G_GRP, 20)])
                    pool.drain().then_inc(ev["taps"], 1)

                group_taps(0)
                cum_steps(layer, 0)

                def scan(g, last):
                    if not last:
                        group_taps(g)
                    pool.wait_ge(ev["y_squares"], ev_n("y_squares", layer, g))
                    settled()
                    row_power(None, TOK, [(TOK, 1.0 / 256)], 8).then_inc(ev["y_rstd"], 1)
                    if not last:
                        pool.wait_ge(full["W1"], fill_n("W1", "seg1", layer, g - 1))
                        settled()
                        cum_steps(layer, g)

                with pool.Fori(1, GROUPS) as g:
                    scan(g, False)
                scan(GROUPS, True)
                with pool.Fori(0, AC_STEPS) as it:
                    load_bias(layer, it)
                norm(2, layer)
                norm(3, layer)
                pool.wait_ge(ev["h_lo"], ev_n("h_lo", layer, 20))
                settled()
                pool.dma_start(pin, ple_in[bass.ts(layer, 1), :, :].rearrange("o p n -> (o p) n")
                               ).then_inc(ple_loaded, 16)
            pool.wait_ge(ev["x_done"], 4 * DEPTH + 1)
            pool.dma_start(fgain, final_gain.partition_broadcast(P)).then_inc(fgain_loaded, 16)
            pool.wait_ge(ev["squares"], 4 * DEPTH + 1)
            row_power(None, TOK, [(TOK, 1.0 / D_MODEL)], 0).then_inc(ev["rstd"], 1)
            pool.wait_ge(final, TOK)
            for t in range(TOK):
                pool.dma_start(out[0, t * P:(t + 1) * P, :], x[:, t, :]).then_inc(out_done, 16)
            pool.wait_ge(out_done, 16 * TOK)

        @block.scalar
        def _(act):
            A = act.activation
            act.preload_act_table_set("exp_and_others")

            def w_split(seg, pos, layer, it=0):
                t, s, count, back = look(seg, pos + AHEAD, it, layer)
                act.wait_ge(arrived[s], count * 16 + 16)
                act.wait_ge(used, t - back + 1 + SLOTS)
                A(w_hi[s][:, :], raw[s][:, :], ACT.Copy).then_inc(hi_done, 1)

            def norm(r, layer, gains=True):
                for t in range(TOK):
                    if t == 0:
                        if gains:
                            act.wait_ge(ev["x_done"], ev_n("x_done", layer, r))
                        act.wait_ge(x_loaded, 16)
                    else:
                        act.drain()
                    i = A(junk, x[:, t, :], ACT.Square, accum_out=stat[:, t:t + 1])
                i.then_inc(ev["squares"], 1)

            def norm_hi(r, layer):
                for b in range(4):
                    act.wait_ge(ev["gained"], ev_n("gained", layer, GAIN_AT[r] + b + 1))
                    A(h_hi[:, 2 * b:2 * b + 2, :], gained[:, b, :].rearrange("p (k t) -> p k t", k=2),
                      ACT.Copy).then_inc(ev["h_hi"], 1)

            def y_split(use, layer, n, src, width):
                act.wait_ge(ev["y_src"], ev_n("y_src", layer, n + Y_AT[use] + 1))
                A(y_hi[:, 0:width, :], src, ACT.Copy).then_inc(ev["y_hi"], 1)

            def ffn(f, layer):
                def chunk(j, c, seg, pos, it=0):
                    b = ("W0", "W1")[c]
                    act.wait_ge(used, done(seg, pos, layer, it))
                    act.wait_ge(ev["y_src"], ev_n("y_src", layer, j + Y_AT[f]))
                    A(ffn_t[:, c, :], bank[b][:, 0:SEQ], ACT.Tanh, scale=0.5).then_inc(ev["ffn_tanh"], 1)

                w_split(f + "pre", 0, layer)
                chunk(0, 0, f + "pre", 1)
                w_split(f + "pre", 1, layer)
                w_split(f + "pre", 2, layer)
                chunk(0, 1, f + "pre", 3)
                w_split(f + "pre", 3, layer)
                y_split(f, layer, 0, act_f, 2)
                with act.Fori(1, PAIRS) as j:
                    w_split(f + "loop", 0, layer, j - 1)
                    chunk(j, 0, f + "loop", 1, j - 1)
                    w_split(f + "loop", 1, layer, j - 1)
                    w_split(f + "loop", 2, layer, j - 1)
                    chunk(j, 1, f + "loop", 3, j - 1)
                    w_split(f + "loop", 3, layer, j - 1)
                    w_split(f + "loop", 4, layer, j - 1)
                    w_split(f + "loop", 5, layer, j - 1)
                    act.wait_ge(used, done(f + "loop", 5, layer, j - 1))
                    y_split(f, layer, j, act_f, 2)
                for k in range(2):
                    w_split(f + "tail", k, layer)

            def first_tiles(layer):
                for k in range(AHEAD):
                    w_split("f1pre", k - AHEAD, layer)

            def conv_evac(layer, g, names, it):
                act.wait_ge(ev["conv"], ev_n("conv", layer, g))
                act.wait_ge(used, done(*names, layer, it))
                A(pre[:, 0:2, 3:3 + SEQ], W0[:, :].rearrange("p (c t) -> p c t", c=2), ACT.Copy
                  ).then_inc(ev["pre_x"], 1)

            def conv_evac2(layer, g, names, it):
                act.wait_ge(used, done(*names, layer, it))
                A(pre[:, 2:4, 3:3 + SEQ], W1[:, :].rearrange("p (c t) -> p c t", c=2), ACT.Copy
                  ).then_inc(ev["pre_bc"], 1)

            def conv_tanh(layer, g):
                act.wait_ge(ev["conv"], ev_n("conv", layer, g + 1))
                A(conv_t, xbc, ACT.Tanh).then_inc(ev["conv_tanh"], 1)

            def z_tanh(layer, g, name, it):
                act.wait_ge(used, done(*name, layer, it))
                act.wait_ge(ev["y_sum"], ev_n("y_sum", layer, g))
                A(zz, W0[:, :].rearrange("p (t c) -> p t c", t=TOK), ACT.Tanh, scale=0.5
                  ).then_inc(ev["z_tanh"], 1)

            def mixer_start(layer):
                split = iter(range(31))

                def w(n):
                    for _ in range(n):
                        w_split("m0", next(split), layer)
                w(2)
                act.wait_ge(used, done("m0", 1, layer))
                act.wait_ge(ev["h_lo"], ev_n("h_lo", layer, 8))
                A(small[:, :, 0:256], W0[:, :].rearrange("p (t c) -> p t c", t=TOK), ACT.Copy
                  ).then_inc(free["W0"], 1)
                w(2)
                act.wait_ge(used, done("m0", 3, layer))
                A(small[:, :, 256:512], W1[:, :].rearrange("p (t c) -> p t c", t=TOK), ACT.Copy
                  ).then_inc(free["W1"], 1)
                act.drain().then_inc(ev["small"], 2)
                for t in range(TOK):
                    A(sq_m0, small[:, t, 0:256], ACT.Square, accum_out=stat[:, 4 + t:5 + t])
                    act.drain()
                for t in range(TOK):
                    A(sq_m0[:, 0:P], small[:, t, 256:384], ACT.Square, accum_out=stat[:, 6 + t:7 + t])
                    act.drain()
                act.drain().then_inc(ev["prep_squares"], 1)
                act.wait_ge(ev["dt_in"], ev_n("dt_in", layer, 1))
                A(prm[:, G_EXPA:G_EXPA + 32], prm[:, G_EXPA:G_EXPA + 32], ACT.Exp)
                A(dt_a[:, 1, :], dt_a[:, 1, :], ACT.Exp, scale=-1.0)
                act.drain()
                A(dt_a[:, 1, :], dt_a[:, 1, :], ACT.Ln, bias=1.0).then_inc(ev["dt_ln"], 1)
                act.preload_act_table_set("exp_and_others")
                for u in range(6):
                    b = ("W0", "W1")[u % 2]
                    w(2)
                    act.wait_ge(used, done("m0", 5 + 2 * u, layer))
                    A(val[:, :, u // 2, (u % 2) * 256:(u % 2) * 256 + 256],
                      bank[b][:, :].rearrange("p (t c) -> p t c", t=TOK), ACT.Copy).then_inc(free[b], 1)
                act.drain().then_inc(ev["v_sb"], 6)
                act.wait_ge(ev["cq_gained"], ev_n("cq_gained", layer, 1))
                act.wait_ge(ev["x_done"], ev_n("x_done", layer, 1))
                A(c_hi[:, :, :], cqf.rearrange("p (k t) -> p k t", k=2), ACT.Copy).then_inc(ev["cq_hi"], 1)
                act.wait_ge(full["S0"], fill_n("S0", "cum", layer))
                A(ecum[:, :], S0[:, 0:32], ACT.Exp)
                A(wl[:, :], S0[:, 32:64], ACT.Exp).then_inc(free["S0"], 1)
                act.drain().then_inc(ev["ecum"], 1)
                for v in range(4):
                    b = ("W0", "W1")[v % 2]
                    w(2)
                    act.wait_ge(used, done("m0", 17 + 2 * v, layer))
                    A(gate_b[:, :, v * 256:v * 256 + 256],
                      bank[b][:, :].rearrange("p (t c) -> p t c", t=TOK), ACT.Tanh, scale=0.5
                      ).then_inc(free[b], 1)
                act.drain().then_inc(ev["gates"], 8)
                w(2)
                conv_evac(layer, 0, ("m0", 25), 0)
                act.drain().then_inc(free["W0"], 1)
                w(2)
                conv_evac2(layer, 0, ("m0", 27), 0)
                act.drain().then_inc(free["W1"], 1)
                act.wait_ge(full["S0"], fill_n("S0", "qi0", layer))
                A(qi[:, 0:2, :], S0[:, :].rearrange("p (h t) -> p h t", h=2), ACT.Copy).then_inc(free["S0"], 1)
                act.wait_ge(used, done("m0", 28, layer))
                A(qi[:, 2:4, :], S1[:, :].rearrange("p (h t) -> p h t", h=2), ACT.Copy).then_inc(free["S1"], 1)
                act.drain().then_inc(ev["qi"], 2)
                w(1)
                conv_tanh(layer, 0)
                for k in range(6):
                    b, name = (("S0", "sc1_even"), ("S1", "sc1_odd"))[k % 2] if k < 4 else \
                        (("S0", "sc0_even"), ("S1", "sc0_odd"))[k % 2]
                    act.wait_ge(full[b], fill_n(b, name, layer, k // 2 if k < 4 else 0))
                    if k >= 2:
                        act.wait_ge(ev["weighted"], ev_n("weighted", layer, k - 1))
                    A(relu[:, k % 2, :], bank[b][:, :], ACT.Relu).then_inc(free[b], 1)
                    act.drain().then_inc(ev["relu"], 1)
                z_tanh(layer, 0, ("m0", 30), 0)

            def scan(layer, g, last):
                sfx = "_last" if last else ""
                q = 0 if last else g - 1
                for t, b in enumerate(("W0", "W1")):
                    act.wait_ge(full[b], fill_n(b, f"seg{t}{sfx}", layer, q))
                    if t == 0:
                        act.wait_ge(ev["xbc"], ev_n("xbc", layer, g))
                    A(decay[:, t, :], bank[b][:, :], ACT.Exp).then_inc(free[b], 1)
                    act.drain().then_inc(ev["decay"], 1)
                for k in (-2, -1):
                    w_split("btail" if last else "bloop", k, layer, q)
                if not last:
                    w_split("bloop", 0, layer, q)
                    w_split("bloop", 1, layer, q)
                    conv_evac(layer, g, ("bloop", 1), q)
                    act.drain().then_inc(free["W0"], 1)
                act.wait_ge(full["S1"], fill_n("S1", f"state{sfx}", layer, q))
                A(st, S1[:, 0:256], ACT.Copy).then_inc(free["S1"], 1)
                act.drain().then_inc(ev["state"], 1)
                act.wait_ge(ev["y_sum"], ev_n("y_sum", layer, g))
                for t in range(TOK):
                    A(sq_b, ysum[:, t, :], ACT.Square, accum_out=stat[:, 8 + t:9 + t])
                    act.drain()
                act.drain().then_inc(ev["y_squares"], 1)
                if not last:
                    w_split("bloop", 2, layer, q)
                    w_split("bloop", 3, layer, q)
                    conv_evac2(layer, g, ("bloop", 3), q)
                    act.drain().then_inc(free["W1"], 1)
                act.wait_ge(used, done("bloop", 7, layer, g - 2))
                y_split("b", layer, g - 1, yt_f[:, :].rearrange("p (k t) -> p k t", k=2), 2)
                if not last:
                    w_split("bloop", 4, layer, q)
                    w_split("bloop", 5, layer, q)
                    conv_tanh(layer, g)
                    z_tanh(layer, g, ("bloop", 5), q)
                else:
                    w_split("btail", 0, layer)
                    w_split("btail", 1, layer)

            def attention(layer, it):
                def w(*ps):
                    for p in ps:
                        w_split("ac", p, layer, it)
                w(0)
                act.wait_ge(ev["y_lo"], ev_n("y_lo", layer, it + Y_AT["a"]))
                act.wait_ge(full["W0"], fill_n("W0", "qa0", layer, it))
                A(qa[:, 0:2, :], W0[:, :].rearrange("p (h t) -> p h t", h=2), ACT.Copy).then_inc(free["W0"], 1)
                act.wait_ge(used, done("ac", 0, layer, it))
                A(qa[:, 2:4, :], W1[:, :].rearrange("p (h t) -> p h t", h=2), ACT.Copy).then_inc(free["W1"], 1)
                act.drain().then_inc(ev["qa"], 1)
                w(1, 2)

                def evacuate_qk(g, b):
                    act.wait_ge(used, done("ac", 2 + 2 * g, layer, it))
                    A(qk[:, g, :, :], bank[b][:, :].rearrange("p (a t) -> p a t", a=2), ACT.Copy
                      ).then_inc(free[b], 1)
                    act.drain().then_inc(ev["qk"], 1)

                evacuate_qk(0, "W0")
                w(3, 4)
                evacuate_qk(1, "W1")
                w(5, 6)
                evacuate_qk(2, "W0")
                w(7)
                act.wait_ge(ev["la"], ev_n("la", layer, it + 1))
                for h in range(4):
                    for t in range(TOK):
                        s = la[:, h, 0:P] if t == 0 else la[:, h, P:3 * P]
                        A(s, s, ACT.Exp, bias=stat[:, 16 + 4 * t + h:17 + 4 * t + h],
                          accum_out=stat[:, 24 + 4 * t + h:25 + 4 * t + h])
                act.drain().then_inc(ev["ea"], 1)
                w(8)
                act.wait_ge(used, done("ac", 8, layer, it))
                A(gate_a[:, :, bass.ts(it, 256)], W1[:, :].rearrange("p (t c) -> p t c", t=TOK), ACT.Tanh,
                  scale=0.5).then_inc(free["W1"], 1)
                for k in range(3):
                    b = ("S1", "S0", "S1")[k]
                    act.wait_ge(full[b], fill_n(b, f"pa{k}", layer, it))
                    A(pa[:, k, :], bank[b][:, :], ACT.Copy).then_inc(free[b], 1)
                    act.drain().then_inc(ev["pa"], 1)
                w(9)
                act.wait_ge(ev["lc"], ev_n("lc", layer, it + 1))
                for e in range(2):
                    for t in range(TOK):
                        s = lc[:, e, :, 0:P] if t == 0 else lc[:, e, :, P:3 * P]
                        k = 2 * t + e
                        A(s, s, ACT.Exp, bias=stat[:, 40 + k:41 + k], accum_out=stat[:, 44 + k:45 + k])
                act.drain().then_inc(ev["ec"], 1)
                w(10)
                act.wait_ge(used, done("ac", 10, layer, it))
                A(gate_c[:, :, bass.ts(it, 256)], W0[:, :].rearrange("p (t c) -> p t c", t=TOK), ACT.Tanh,
                  scale=0.5).then_inc(free["W0"], 1)
                act.drain().then_inc(ev["gates"], 2)
                act.wait_ge(used, done("ac", 14, layer, it - 1))
                y_split("a", layer, it, qa, 4)
                for k in range(5):
                    b = ("S0", "S1")[k % 2]
                    n = 4 if k < 4 else 2
                    act.wait_ge(full[b], fill_n(b, f"pc{k}", layer, it))
                    A(pc[:, 4 * k:4 * k + n, :], bank[b][:, 0:n * P].rearrange("p (a t) -> p a t", a=n), ACT.Copy
                      ).then_inc(free[b], 1)
                    act.drain().then_inc(ev["pc"], 1)
                w(11, 12, 13)
                act.wait_ge(full["S0"], fill_n("S0", "ocT", layer, it))
                A(yc_t[:, bass.ts(it, 1), :], S0[:, 0:SEQ].unsqueeze(1), ACT.Copy).then_inc(free["S0"], 1)
                act.drain().then_inc(ev["oc"], 1)
                w(14)

            with act.Fori(0, DEPTH) as layer:
                first_tiles(layer)
                norm(0, layer)
                norm_hi(0, layer)
                ffn("f1", layer)
                norm(1, layer)
                norm_hi(1, layer)
                mixer_start(layer)
                with act.Fori(1, GROUPS) as g:
                    scan(layer, g, False)
                scan(layer, GROUPS, True)
                with act.Fori(0, AC_STEPS) as it:
                    attention(layer, it)
                act.drain().then_inc(ev["y_src"], 1)
                act.wait_ge(used, done("ac", 14, layer, AC_STEPS - 1))
                A(y_hi[:, 0:4, :], yc_t[:, :, :], ACT.Copy).then_inc(ev["y_hi"], 1)
                for k in range(4):
                    w_split("out", k, layer)
                for b in range(4):
                    act.wait_ge(ev["gained"], ev_n("gained", layer, 8 + b + 1))
                    A(h_hi[:, 2 * b:2 * b + 2, :], mg[:, b, :].rearrange("p (k t) -> p k t", k=2),
                      ACT.Copy).then_inc(ev["h_hi"], 1)
                for k in range(4, 12):
                    w_split("out", k, layer)
                norm(2, layer)
                norm_hi(2, layer)
                ffn("f2", layer)
                norm(3, layer)
                norm_hi(3, layer)
                for k in range(6):
                    w_split("ple", k, layer)
                act.wait_ge(ple_loaded, layer * 16 + 16)
                A(c_hi[:, :, :], pin.rearrange("p (k t) -> p k t", k=2), ACT.Copy).then_inc(ev["cq_hi"], 1)
                for k, b in enumerate(("W0", "W1", "S0", "S1")):
                    act.wait_ge(used, done("ple", 2 * k + 1, layer))
                    A(pg[:, :, k * 256:k * 256 + 256], bank[b][:, :].rearrange("p (t c) -> p t c", t=TOK),
                      ACT.Tanh, scale=0.5).then_inc(free[b], 1)
                act.drain().then_inc(ev["gates"], 4)
            act.wait_ge(ev["x_done"], 4 * DEPTH + 1)
            norm(4, 0, gains=False)

        @block.vector
        def _(dve):
            TT, TS, STT = dve.tensor_tensor, dve.tensor_scalar, dve.scalar_tensor_tensor

            def w_split(seg, pos, layer, it=0):
                t, s, _, _ = look(seg, pos + AHEAD, it, layer)
                dve.wait_ge(hi_done, t + 1)
                TT(w_lo[s][:, :], raw[s][:, :], w_hi[s][:, :].bitcast(f32), SUB).then_inc(lo_done, 1)

            def norm(r, layer):
                dve.wait_ge(ev["rstd"], ev_n("rstd", layer, r + 1))
                for t in range(TOK):
                    TS(xn[:, t, :], x[:, t, :], stat[:, t:t + 1], None, MUL)
                dve.drain().then_inc(ev["xn"], 1)

            def norm_gain(r, layer):
                if r == 0:
                    dve.wait_ge(prm_loaded, layer * 16 + 16)
                for k, b in enumerate(("W0", "W1", "S0", "S1")):
                    dve.wait_ge(full[b], fill_n(b, f"norm{r}", layer))
                    gain = prm[:, G_NORM + 8 * r + 2 * k:G_NORM + 8 * r + 2 * k + 2]
                    TT(gained[:, k, :].rearrange("p (k t) -> p k t", k=2),
                       bank[b][:, :].rearrange("p (k t) -> p k t", k=2),
                       gain.unsqueeze(2).broadcast_to([P, 2, SEQ]), MUL).then_inc(free[b], 1)
                    dve.drain().then_inc(ev["gained"], 1)
                for b in range(4):
                    h_lo_part(b, layer, GAIN_AT[r], gained)

            def h_lo_part(b, layer, first, src):
                dve.wait_ge(ev["h_hi"], ev_n("h_hi", layer, first + b + 1))
                TT(h_lo[:, 2 * b:2 * b + 2, :], src[:, b, :].rearrange("p (k t) -> p k t", k=2),
                   h_hi[:, 2 * b:2 * b + 2, :].bitcast(f32), SUB).then_inc(ev["h_lo"], 1)

            def y_split(use, layer, n, src, width):
                dve.wait_ge(ev["y_hi"], ev_n("y_hi", layer, n + Y_AT[use] + 1))
                TT(y_lo[:, 0:width, :], src, y_hi[:, 0:width, :].bitcast(f32), SUB).then_inc(ev["y_lo"], 1)

            def residual(seg, pos, layer, scale):
                dve.wait_ge(used, done(seg, pos, layer))
                for t in range(TOK):
                    for h in range(2):
                        STT(x[:, t, 512 * h:512 * h + 512], acc[t][h][:, :], scale,
                            x[:, t, 512 * h:512 * h + 512], MUL, ADD)
                dve.drain().then_inc(ev["acc_free"], 1)
                dve.drain().then_inc(ev["x_done"], 1)

            def ffn(f, layer):
                def chunk(j, c, seg, pos, it=0):
                    b = ("W0", "W1")[c]
                    first = 0 if f == "f1" else 2 * PAIRS
                    dve.wait_ge(ev["ffn_tanh"], ev_n("ffn_tanh", layer, j * 2 + (first + c + 1)))
                    STT(ffn_t[:, c, :], ffn_t[:, c, :], 1.0, bank[b][:, 0:SEQ], ADD, MUL)
                    dve.drain()
                    dve.wait_ge(used, done(seg, pos, layer, it))
                    STT(act_f[:, c, :], ffn_t[:, c, :], 0.5, bank[b][:, SEQ:512], MUL, MUL
                        ).then_inc(free[b], 1)

                w_split(f + "pre", 0, layer)
                w_split(f + "pre", 1, layer)
                chunk(0, 0, f + "pre", 1)
                w_split(f + "pre", 2, layer)
                w_split(f + "pre", 3, layer)
                chunk(0, 1, f + "pre", 3)
                dve.drain().then_inc(ev["y_src"], 1)
                y_split(f, layer, 0, act_f, 2)
                with dve.Fori(1, PAIRS) as j:
                    w_split(f + "loop", 0, layer, j - 1)
                    w_split(f + "loop", 1, layer, j - 1)
                    dve.drain()
                    chunk(j, 0, f + "loop", 1, j - 1)
                    w_split(f + "loop", 2, layer, j - 1)
                    w_split(f + "loop", 3, layer, j - 1)
                    chunk(j, 1, f + "loop", 3, j - 1)
                    dve.drain().then_inc(ev["y_src"], 1)
                    w_split(f + "loop", 4, layer, j - 1)
                    w_split(f + "loop", 5, layer, j - 1)
                    y_split(f, layer, j, act_f, 2)
                for k in range(2):
                    w_split(f + "tail", k, layer)
                residual(f + "tail", 1, layer, 0.5)

            def conv(layer, g, first):
                if first == 0:
                    dve.wait_ge(ev["taps"], ev_n("taps", layer, g + 1))
                    dve.wait_ge(ev["pre_x"], ev_n("pre_x", layer, g + 1))
                else:
                    dve.wait_ge(ev["pre_bc"], ev_n("pre_bc", layer, g + 1))
                for c in range(first, first + 2):
                    TS(xbc[:, c, :], pre[:, c, 0:SEQ], taps[:, 4 * c:4 * c + 1], taps[:, 16 + c:17 + c], MUL, ADD)
                for k in range(1, 4):
                    dve.drain()
                    for c in range(first, first + 2):
                        STT(xbc[:, c, :], pre[:, c, k:k + SEQ], taps[:, 4 * c + k:4 * c + k + 1], xbc[:, c, :],
                            MUL, ADD)
                if first == 2:
                    dve.drain().then_inc(ev["conv"], 1)

            def conv_silu(layer, g):
                dve.wait_ge(ev["conv_tanh"], ev_n("conv_tanh", layer, g + 1))
                STT(xbc, conv_t, 1.0, xbc, ADD, MUL)
                dve.drain().then_inc(ev["xbc"], 1)

            def gate_z(layer, g):
                dve.wait_ge(ev["z_tanh"], ev_n("z_tanh", layer, g + 1))
                STT(zz, zz, 1.0, W0[:, :].rearrange("p (t c) -> p t c", t=TOK), ADD, MUL
                    ).then_inc(free["W0"], 1)
                dve.drain().then_inc(ev["zz"], 1)

            def mixer_start(layer):
                split = iter(range(31))

                def w(n):
                    for _ in range(n):
                        w_split("m0", next(split), layer)
                grp = prm[:, G_GRP:G_GRP + GROUPS * GRP].rearrange("p (g n) -> p g n", g=GROUPS)[:, :, 0:20]
                TS(grp, grp, 0.5, None, MUL)
                w(4)
                dve.drain()
                dve.wait_ge(ev["small"], ev_n("small", layer, 2))
                TT(dt_a[:, 0, :].rearrange("p (t h) -> p t h", t=TOK), small[:, :, 456:488],
                   prm[:, G_DTB:G_DTB + 32].unsqueeze(1).broadcast_to([P, TOK, 32]), ADD)
                dve.tensor_copy(ki2.rearrange("p t (e c) -> p t e c", e=2),
                                small[:, :, 384:448].unsqueeze(2).broadcast_to([P, TOK, 2, IDX_DIM]))
                TS(wix[:, :, :], small[:, :, 448:456], float((IDX_HEADS * IDX_DIM) ** -0.5), None, MUL)
                dve.drain()
                STT(dt_a[:, 1, :], dt_a[:, 0, :], -1.0, dt_a[:, 0, :], MUL, MAX)
                dve.drain().then_inc(ev["dt_in"], 1)
                w(2)
                dve.wait_ge(ev["prep_rstd"], ev_n("prep_rstd", layer, 1))
                for t in range(TOK):
                    TS(cqn[:, t, :], small[:, t, 0:256], stat[:, 4 + t:5 + t], None, MUL)
                    TS(kvn[:, t, :], small[:, t, 256:384], stat[:, 6 + t:7 + t], None, MUL)
                dve.drain().then_inc(ev["prep_n"], 1)
                w(2)
                dve.wait_ge(ev["dt_ln"], ev_n("dt_ln", layer, 1))
                STT(dts[:, :, :].rearrange("p t h -> p (t h)"), dt_a[:, 0, :], 0.0, dt_a[:, 1, :], MAX, ADD)
                dve.drain()
                STT(da[:, :, :], dts[:, :, :], -1.0,
                    prm[:, G_EXPA:G_EXPA + 32].unsqueeze(1).broadcast_to([P, TOK, 32]), MUL, MUL)
                dve.drain().then_inc(ev["da"], 1)
                w(8)
                dve.wait_ge(full["S0"], fill_n("S0", "cqT", layer))
                TT(cqf.rearrange("p (k t) -> p k t", k=2), S0[:, :].rearrange("p (k t) -> p k t", k=2),
                   prm[:, G_CQ:G_CQ + 2].unsqueeze(2).broadcast_to([P, 2, SEQ]), MUL).then_inc(free["S0"], 1)
                dve.drain().then_inc(ev["cq_gained"], 1)
                dve.wait_ge(full["S1"], fill_n("S1", "kvT", layer))
                TS(kv_t[:, :], S1[:, 0:SEQ], prm[:, G_CKV:G_CKV + 1], None, MUL)
                dve.tensor_copy(ki_t[:, :], S1[:, SEQ:512]).then_inc(free["S1"], 1)
                dve.drain().then_inc(ev["kv"], 1)
                dve.wait_ge(ev["cq_hi"], ev_n("cq_hi", layer, 1))
                TT(c_lo[:, :, :], cqf.rearrange("p (k t) -> p k t", k=2), c_hi[:, :, :].bitcast(f32), SUB
                   ).then_inc(ev["cq_lo"], 1)
                w(12)
                conv(layer, 0, 0)
                conv(layer, 0, 2)
                w(1)
                conv_silu(layer, 0)
                for k in range(6):
                    dve.wait_ge(ev["relu"], ev_n("relu", layer, k + 1))
                    heads, width, at, t = indexer_fill(k)
                    for e, h in enumerate(heads):
                        acc_in = causal if h == 0 else score
                        STT(score[:, at:at + width], relu[:, k % 2, e * width:(e + 1) * width],
                            wix[:, t, h:h + 1], acc_in[:, at:at + width], MUL, ADD)
                        dve.drain()
                    dve.drain().then_inc(ev["weighted"], 1)
                gate_z(layer, 0)

            def top_round(layer):
                for t, (a, n) in enumerate(((0, P), (P, SEQ))):
                    dve.max(top8[:, t, :], score[:, a:a + n])
                dve.drain()
                for t, (a, n) in enumerate(((0, P), (P, SEQ))):
                    dve.match_replace(out=score[:, a:a + n], in_to_replace=top8[:, t, :],
                                      in_values=score[:, a:a + n], imm_value=SCORE_TAKEN)
                dve.drain()

            def scan(layer, g, last):
                sfx = "_last" if last else ""
                q = 0 if last else g - 1
                gi = g - 1
                S0g = S0[:, :].rearrange("p (t h c) -> p t h c", t=TOK, h=HG)
                hd = [P, TOK, HG, HEADDIM]
                heads = bass.ts(gi, HG)
                if last:
                    dve.wait_ge(ev["ecum"], ev_n("ecum", layer, 1))
                dve.wait_ge(full["S0"], fill_n("S0", f"xT{sfx}", layer, q))
                xdt4 = xdt.rearrange("p t (h c) -> p t h c", h=HG)
                xd4 = xd.rearrange("p t (h c) -> p t h c", h=HG)
                skip = prm[:, bass.ds(gi * GRP + (G_GRP + 22), 4)]
                TT(xdt4, S0g, dts[:, :, heads].unsqueeze(3).broadcast_to(hd), MUL)
                TT(xd4, S0g, skip.unsqueeze(1).unsqueeze(3).broadcast_to(hd), MUL).then_inc(free["S0"], 1)
                dve.wait_ge(full["S1"], fill_n("S1", f"bcb{sfx}", layer, q))
                dve.tensor_copy(b_tok, S1[:, 0:P])
                TT(cbm, S1[:, P:3 * P].rearrange("p (t i) -> p t i", t=TOK),
                   upto[:, :].unsqueeze(1).broadcast_to([P, TOK, P]), MUL).then_inc(free["S1"], 1)
                dve.drain()
                TT(xw.rearrange("p (h c) -> p h c", h=HG), xdt4[:, 0, :, :],
                   wl[:, heads].unsqueeze(2).broadcast_to([P, HG, HEADDIM]), MUL)
                dve.drain().then_inc(ev["ssd_in"], 1)
                for t in range(TOK):
                    dve.wait_ge(ev["decay"], ev_n("decay", layer, gi * 2 + t + 1))
                    d4 = decay[:, t, :].rearrange("p (h i) -> p h i", h=HG)
                    TT(d4, d4, cbm[:, t, :].unsqueeze(1).broadcast_to([P, HG, P]), MUL)
                dve.drain().then_inc(ev["scan_w"], 1)
                for k in (-2, -1):
                    w_split("btail" if last else "bloop", k, layer, q)
                if not last:
                    w_split("bloop", 0, layer, q)
                    w_split("bloop", 1, layer, q)
                top_round(layer)
                dve.wait_ge(full["S0"], fill_n("S0", f"ydiag{sfx}", layer, q))
                TT(ysum, S0[:, :].rearrange("p (t c) -> p t c", t=TOK), xd, ADD).then_inc(free["S0"], 1)
                dve.wait_ge(full["S1"], fill_n("S1", f"yoff{sfx}", layer, q))
                TT(yoffs.rearrange("p (h c) -> p h c", h=HG), S1[:, 0:256].rearrange("p (h c) -> p h c", h=HG),
                   ecum[:, heads].unsqueeze(2).broadcast_to([P, HG, HEADDIM]), MUL).then_inc(free["S1"], 1)
                dve.drain()
                TT(ysum[:, 1, :], ysum[:, 1, :], yoffs, ADD)
                dve.drain()
                STT(ysum, zz, 0.5, ysum, MUL, MUL)
                dve.drain().then_inc(ev["y_sum"], 1)
                if not last:
                    w_split("bloop", 2, layer, q)
                dve.wait_ge(ev["y_rstd"], ev_n("y_rstd", layer, g))
                for t in range(TOK):
                    TS(ysum[:, t, :], ysum[:, t, :], stat[:, 8 + t:9 + t], None, MUL)
                dve.drain().then_inc(ev["yn"], 1)
                if not last:
                    conv(layer, g, 0)
                    w_split("bloop", 3, layer, q)
                dve.wait_ge(full["S1"], fill_n("S1", f"yT{sfx}", layer, q))
                gain = prm[:, bass.ds(gi * GRP + (G_GRP + 20), 2)]
                TT(yt_f[:, :].rearrange("p (k t) -> p k t", k=2), S1[:, :].rearrange("p (k t) -> p k t", k=2),
                   gain.unsqueeze(2).broadcast_to([P, 2, SEQ]), MUL).then_inc(free["S1"], 1)
                dve.drain().then_inc(ev["y_src"], 1)
                y_split("b", layer, gi, yt_f[:, :].rearrange("p (k t) -> p k t", k=2), 2)
                if not last:
                    conv(layer, g, 2)
                    w_split("bloop", 4, layer, q)
                    w_split("bloop", 5, layer, q)
                    conv_silu(layer, g)
                    gate_z(layer, g)
                else:
                    w_split("btail", 0, layer)
                    w_split("btail", 1, layer)

            def gated(layer, gate, gates_at):
                dve.wait_ge(ev["gates"], ev_n("gates", layer, gates_at))
                for t in range(TOK):
                    for h in range(2):
                        c = slice(512 * h, 512 * h + 512)
                        STT(gate[:, t, c], gate[:, t, c], 1.0, acc[t][h][:, :], ADD, MUL)
                dve.drain().then_inc(ev["acc_free"], 1)

            def attention(layer, it):
                def w(*ps):
                    for p in ps:
                        w_split("ac", p, layer, it)
                w(0, 1, 2)
                dve.drain()
                dve.wait_ge(bias_loaded, layer * (64 * AC_STEPS) + (it * 64 + 64))
                dve.wait_ge(ev["pc"], ev_n("pc", layer, it * 5))
                scale = float(A_DC ** -0.5)
                for k, (b, hs) in enumerate((("S0", 0), ("S1", 2))):
                    dve.wait_ge(full[b], fill_n(b, f"la{k}", layer, it))
                    STT(la[:, hs:hs + 2, P:3 * P], bank[b][:, :].rearrange("p (h s) -> p h s", h=2), scale,
                        bias[:, hs:hs + 2, :], MUL, ADD).then_inc(free[b], 1)
                w(3, 4)
                dve.wait_ge(full["S0"], fill_n("S0", "la2", layer, it))
                STT(la[:, :, 0:P], S0[:, :].rearrange("p (h s) -> p h s", h=4), scale,
                    bias[:, 0:4, P:SEQ], MUL, ADD).then_inc(free["S0"], 1)
                dve.drain()
                TT(la, la, score[:, :].unsqueeze(1).broadcast_to([P, 4, 3 * P]), ADD)
                dve.drain()
                for t in range(TOK):
                    s = la[:, :, 0:P] if t == 0 else la[:, :, P:3 * P]
                    dve.tensor_reduce(stat[:, 16 + 4 * t:20 + 4 * t], s, AX.X, MAX)
                dve.drain()
                TS(stat[:, 16:24], stat[:, 16:24], -1.0, None, MUL)
                dve.drain().then_inc(ev["la"], 1)
                w(5, 6)
                scale = float(C_DIM ** -0.5)
                for g in range(CG):
                    for e, b in enumerate(("S0", "S1")):
                        dve.wait_ge(full[b], fill_n(b, f"lc{2 * g + e}", layer, it))
                        STT(lc[:, e, g, 0:P], bank[b][:, 0:P], scale, bias[:, 4 + 2 * g + e, P:SEQ], MUL, ADD)
                        STT(lc[:, e, g, P:3 * P], bank[b][:, P:3 * P], scale, bias[:, 4 + 2 * g + e, :],
                            MUL, ADD).then_inc(free[b], 1)
                dve.wait_ge(ev["ea"], ev_n("ea", layer, it + 1))
                dve.reciprocal(stat[:, 32:40], stat[:, 24:32])
                dve.drain()
                for t in range(TOK):
                    s, n = (la[:, :, 0:P], P) if t == 0 else (la[:, :, P:3 * P], SEQ)
                    TT(s, s, stat[:, 32 + 4 * t:36 + 4 * t].unsqueeze(2).broadcast_to([P, 4, n]), MUL)
                dve.drain().then_inc(ev["na"], 1)
                w(7)
                for e in range(2):
                    for t in range(TOK):
                        s = lc[:, e, :, 0:P] if t == 0 else lc[:, e, :, P:3 * P]
                        dve.tensor_reduce(stat[:, 40 + 2 * t + e:41 + 2 * t + e], s, AX.XY, MAX)
                dve.drain()
                TS(stat[:, 40:44], stat[:, 40:44], -1.0, None, MUL)
                dve.drain().then_inc(ev["lc"], 1)
                w(8, 9)
                for t, b in enumerate(("S0", "S1")):
                    dve.wait_ge(full[b], fill_n(b, f"oa{t}", layer, it))
                    TS(qa[:, :, t * P:(t + 1) * P], bank[b][:, :].rearrange("p (h q) -> p h q", h=4),
                       prm[:, G_CKV:G_CKV + 1], None, MUL).then_inc(free[b], 1)
                dve.drain().then_inc(ev["y_src"], 1)
                w(10)
                y_split("a", layer, it, qa, 4)
                dve.wait_ge(ev["ec"], ev_n("ec", layer, it + 1))
                dve.reciprocal(stat[:, 48:52], stat[:, 44:48])
                w(11, 12)
                dve.drain()
                dve.wait_ge(full["S1"], fill_n("S1", "oc", layer, it))
                TT(oc_f.rearrange("p t (e c) -> p t e c", e=2),
                   S1[:, 0:2 * P].rearrange("p (t e c) -> p t e c", t=TOK, e=2),
                   stat[:, 48:52].rearrange("p (t e) -> p t e", t=TOK).unsqueeze(3)
                   .broadcast_to([P, TOK, 2, C_DIM]), MUL).then_inc(free["S1"], 1)
                dve.drain().then_inc(ev["nc_"], 1)
                w(13, 14)

            dve.sem_inc(lo_done, SLOTS)
            for name in SEEDED:
                dve.sem_inc(ev[name], 1)
            for b in bank:
                dve.sem_inc(free[b], 1)
            dve.memset(pre[:, :, 0:3], 0.0)
            for v in range(4):
                n = A_HEADS if v == 0 else C_HEADS
                dve.wait_ge(tables, v + 1)
                dve.tensor_copy(rb[0:n, v, :], acc[v // 2][v % 2][0:n, 0:ROW]).then_inc(tables_sb, 1)

            with dve.Fori(0, DEPTH) as layer:
                for k in range(AHEAD):
                    w_split("f1pre", k - AHEAD, layer)
                dve.wait_ge(x_loaded, 16)
                norm(0, layer)
                norm_gain(0, layer)
                ffn("f1", layer)
                norm(1, layer)
                norm_gain(1, layer)
                dve.drain()
                dve.memset(pre[:, :, 0:3], 0.0)
                mixer_start(layer)
                with dve.Fori(1, GROUPS) as g:
                    scan(layer, g, False)
                scan(layer, GROUPS, True)
                TS(score[:, :], score[:, :], SCORE_CUT, MASKED, ALU.is_ge, MUL)
                dve.wait_ge(used, done("btail", 1, layer))
                gated(layer, gate_b, 8)
                with dve.Fori(0, AC_STEPS) as it:
                    attention(layer, it)
                dve.wait_ge(ev["branch_a"], ev_n("branch_a", layer, 1))
                gated(layer, gate_a, 8 + 2 * AC_STEPS)
                dve.wait_ge(ev["oc"], ev_n("oc", layer, AC_STEPS))
                y_split("c", layer, 0, yc_t[:, :, :], 4)
                for k in range(4):
                    w_split("out", k, layer)
                dve.wait_ge(used, done("out", 3, layer))
                gated(layer, gate_c, 8 + 2 * AC_STEPS)
                for g in (gate_a, gate_c):
                    dve.drain()
                    TT(gate_b[:, :, :], gate_b[:, :, :], g[:, :, :], ADD)
                dve.drain().then_inc(ev["merged"], 1)
                for b, nm in enumerate(("W0", "W1", "S0", "S1")):
                    dve.wait_ge(full[nm], fill_n(nm, "mT", layer))
                    TS(mg[:, b, :], bank[nm][:, :], 0.5, None, MUL).then_inc(free[nm], 1)
                    dve.drain().then_inc(ev["gained"], 1)
                for b in range(4):
                    h_lo_part(b, layer, 8, mg)
                for k in range(4, 12):
                    w_split("out", k, layer)
                residual("out", 11, layer, 1.0)
                norm(2, layer)
                norm_gain(2, layer)
                ffn("f2", layer)
                norm(3, layer)
                norm_gain(3, layer)
                for k in range(6):
                    w_split("ple", k, layer)
                dve.wait_ge(ev["cq_hi"], ev_n("cq_hi", layer, 2))
                TT(c_lo[:, :, :], pin.rearrange("p (k t) -> p k t", k=2), c_hi[:, :, :].bitcast(f32), SUB
                   ).then_inc(ev["cq_lo"], 1)
                dve.wait_ge(ev["gates"], ev_n("gates", layer, 20))
                dve.wait_ge(used, done("ple", 9, layer))
                for t in range(TOK):
                    for h in range(2):
                        c = slice(512 * h, 512 * h + 512)
                        STT(pg[:, t, c], pg[:, t, c], 1.0, acc[t][h][:, :], ADD, MUL)
                dve.drain().then_inc(ev["acc_free"], 1)
                STT(x[:, :, :], pg, 0.5, x[:, :, :], MUL, ADD)
                dve.drain().then_inc(ev["x_done"], 1)
            dve.wait_ge(ev["rstd"], 4 * DEPTH + 1)
            dve.wait_ge(fgain_loaded, 16)
            for t in range(TOK):
                STT(x[:, t, :], x[:, t, :], stat[:, t:t + 1], fgain, MUL, MUL).then_inc(final, 1)

        @block.tensor
        def _(pe):
            mm = pe.matmul

            def three(o, lh, ll, rh, rl, start, stop):
                mm(o, lh, rh, start=start, stop=False)
                mm(o, lh, rl, start=False, stop=False)
                return mm(o, ll, rh, start=False, stop=stop)

            def weight(seg, pos, layer, it=0):
                t, s, _, _ = tile_numbers(seg, pos, it, layer)
                pe.wait_ge(lo_done, t + 1 + SLOTS)
                return s

            def fill(b, name, layer, it=0):
                pe.wait_ge(free[b], free_n(b, name, layer, it))
                return bank[b]

            def features(o, seg, pos, layer, it=0):
                s = weight(seg, pos, layer, it)
                for k in range(KD):
                    c = slice(k * P, (k + 1) * P)
                    last = three(o, w_hi[s][:, c], w_lo[s][:, c], h_hi[:, k, :], h_lo[:, k, :],
                                 k == 0, k == KD - 1)
                last.then_inc(used, 1)
                return last

            def tokens(b, seg, pos, layer, it=0):
                s = [weight(seg, pos + i, layer, it) for i in range(2)]
                for t in range(TOK):
                    for k in range(KD):
                        sl, c = s[k // 4], slice((k % 4) * 256, (k % 4) * 256 + 256)
                        o = b[:, t * 256:t * 256 + 256]
                        hh, hl = (a[:, k, t * P:(t + 1) * P] for a in (h_hi, h_lo))
                        mm(o, hh, w_hi[sl][:, c], start=k == 0, stop=False)
                        mm(o, hh, w_lo[sl][:, c], start=False, stop=False)
                        last = mm(o, hl, w_hi[sl][:, c], start=False, stop=k == KD - 1)
                        if t == TOK - 1 and k % 4 == 3:
                            last.then_inc(used, 1)

            def rows(yh, yl, seg, pos, layer, it=0, start=False, stop=False):
                s = weight(seg, pos, layer, it)
                for t in range(TOK):
                    a, b = yh[:, t * P:(t + 1) * P], yl[:, t * P:(t + 1) * P]
                    for h in range(2):
                        c = slice(512 * h, 512 * h + 512)
                        mm(acc[t][h][:, :], a, w_hi[s][:, c], start=start, stop=False)
                        mm(acc[t][h][:, :], a, w_lo[s][:, c], start=False, stop=False)
                        last = mm(acc[t][h][:, :], b, w_hi[s][:, c], start=False, stop=stop)
                last.then_inc(used, 1)

            def acc_zero(use, layer):
                pe.wait_ge(ev["acc_free"], ev_n("acc_free", layer, ACC_USES[use]))
                for t in range(TOK):
                    for h in range(2):
                        mm(acc[t][h][:, :], zeros[:, 0:P], zeros[:, :], start=True, stop=False)

            def turn_rows(src, name, layer):
                for b, nm in enumerate(("W0", "W1", "S0", "S1")):
                    o = fill(nm, name, layer)
                    for k in range(2):
                        for t in range(TOK):
                            c = (2 * b + k) * P
                            last = pe.transpose(o[:, k * SEQ + t * P:k * SEQ + (t + 1) * P],
                                                src[:, t, c:c + P], ident[:, :])
                    last.then_inc(full[nm], 1)

            def norm(r, layer):
                pe.wait_ge(ev["xn"], ev_n("xn", layer, r + 1))
                turn_rows(xn, f"norm{r}", layer)
                pe.wait_ge(ev["h_lo"], ev_n("h_lo", layer, GAIN_AT[r] + 4))

            def ffn(f, layer):
                def chunk(seg, pos, j, c, it=0):
                    b, name = (("W0", f + "even"), ("W1", f + "odd"))[c]
                    o = fill(b, name, layer, j)
                    features(o[:, 0:SEQ], seg, pos, layer, it)
                    features(o[:, SEQ:512], seg, pos + 1, layer, it)

                def down(seg, pos, j, it=0, stop=False):
                    pe.wait_ge(ev["y_lo"], ev_n("y_lo", layer, j + (Y_AT[f] + 1)))
                    for k in range(2):
                        rows(y_hi[:, k, :], y_lo[:, k, :], seg, pos + k, layer, it, stop=stop and k == 1)

                acc_zero(f, layer)
                chunk(f + "pre", 0, 0, 0)
                chunk(f + "pre", 2, 0, 1)
                with pe.Fori(1, PAIRS) as j:
                    chunk(f + "loop", 0, j, 0, j - 1)
                    chunk(f + "loop", 2, j, 1, j - 1)
                    down(f + "loop", 4, j - 1, j - 1)
                down(f + "tail", 0, PAIRS - 1, stop=True)

            def project_x(name, seg, pos, layer, it=0):
                o = fill("W0", name, layer, it)
                features(o[:, 0:SEQ], seg, pos, layer, it)
                features(o[:, SEQ:512], seg, pos + 1, layer, it)

            def project_bc(name, seg, pos, layer, it=0):
                o = fill("W1", name, layer, it)
                features(o[:, 0:SEQ], seg, pos, layer, it)
                features(o[:, SEQ:512], seg, pos + 1, layer, it)

            def project_tok(b, name, seg, pos, layer, it=0):
                o = fill(b, name, layer, it)
                tokens(o, seg, pos, layer, it)

            def mixer_start(layer):
                project_tok("W0", "small0", "m0", 0, layer)
                project_tok("W1", "small1", "m0", 2, layer)
                for u in range(6):
                    b, name = (("W0", "v_even"), ("W1", "v_odd"))[u % 2]
                    tokens_at(b, name, "m0", 4 + 2 * u, layer, u // 2)
                pe.wait_ge(ev["prep_n"], ev_n("prep_n", layer, 1))
                o = fill("S0", "cqT", layer)
                for k in range(2):
                    for t in range(TOK):
                        last = pe.transpose(o[:, k * SEQ + t * P:k * SEQ + (t + 1) * P],
                                            cqn[:, t, k * P:(k + 1) * P], ident[:, :])
                last.then_inc(full["S0"], 1)
                o = fill("S1", "kvT", layer)
                for t in range(TOK):
                    pe.transpose(o[:, t * P:(t + 1) * P], kvn[:, t, :], ident[:, :])
                for t in range(TOK):
                    last = pe.transpose(o[:, SEQ + t * P:SEQ + (t + 1) * P], ki2[:, t, :], ident[:, :])
                last.then_inc(full["S1"], 1)
                pe.wait_ge(ev["da"], ev_n("da", layer, 1))
                o = fill("S0", "cum", layer)
                mm(o[:, 0:32], upto[:, :], da[:, 1, :], start=True, stop=True)
                mm(o[:, 32:64], after[:, :], da[:, 0, :], start=True, stop=True).then_inc(full["S0"], 1)
                for v in range(4):
                    b, name = (("W0", "gb_even"), ("W1", "gb_odd"))[v % 2]
                    tokens_at(b, name, "m0", 16 + 2 * v, layer, v // 2)
                project_x("x_first", "m0", 24, layer)
                project_bc("bc_first", "m0", 26, layer)
                pe.wait_ge(ev["cq_lo"], ev_n("cq_lo", layer, 1))
                s = weight("m0", 28, layer)
                for c, b in enumerate(("S0", "S1")):
                    o = fill(b, f"qi{c}", layer)
                    for e in range(2):
                        for kk in range(2):
                            at = kk * 512 + (2 * c + e) * P
                            cs = slice(at, at + P)
                            last = three(o[:, e * SEQ:(e + 1) * SEQ], w_hi[s][:, cs], w_lo[s][:, cs],
                                         c_hi[:, kk, :], c_lo[:, kk, :], kk == 0, kk == 1)
                    last.then_inc(full[b] if c == 0 else used, 1)
                pe.wait_ge(ev["qi"], ev_n("qi", layer, 2))
                pe.wait_ge(ev["kv"], ev_n("kv", layer, 1))
                for k in range(6):
                    b, name = (("S0", "sc1_even"), ("S1", "sc1_odd"))[k % 2] if k < 4 else \
                        (("S0", "sc0_even"), ("S1", "sc0_odd"))[k % 2]
                    o = fill(b, name, layer, k // 2 if k < 4 else 0)
                    heads, width, _, t = indexer_fill(k)
                    r = slice((k % 2) * IDX_DIM, (k % 2 + 1) * IDX_DIM)
                    for e, h in enumerate(heads):
                        last = mm(o[:, e * width:(e + 1) * width], qi[r, h // 2, t * P:(t + 1) * P],
                                  ki_t[r, 0:width], start=True, stop=True)
                    last.then_inc(full[b], 1)
                    if k == 1:
                        tokens_at("W0", "z_first", "m0", 29, layer)

            def tokens_at(b, name, seg, pos, layer, it=0):
                o = fill(b, name, layer, it)
                tokens(o, seg, pos, layer)

            def scan(layer, g, last):
                sfx = "_last" if last else ""
                q = 0 if last else g - 1
                gi = g - 1
                pe.wait_ge(ev["dau"], ev_n("dau", layer, g))
                for t, b in enumerate(("W0", "W1")):
                    o = fill(b, f"seg{t}{sfx}", layer, q)
                    mm(o[:, :], after[:, :], dau[:, t, :], start=True, stop=True).then_inc(full[b], 1)
                pe.wait_ge(ev["xbc"], ev_n("xbc", layer, g))
                o = fill("S0", f"xT{sfx}", layer, q)
                for t in range(TOK):
                    for c in range(2):
                        i = pe.transpose(o[:, t * 256 + c * P:t * 256 + (c + 1) * P],
                                         xbc[:, c, t * P:(t + 1) * P], ident[:, :])
                i.then_inc(full["S0"], 1)
                o = fill("S1", f"bcb{sfx}", layer, q)
                pe.transpose(o[:, 0:P], xbc[:, 2, 0:P], ident[:, :])
                for t in range(TOK):
                    ts = slice(t * P, (t + 1) * P)
                    i = mm(o[:, P + t * P:2 * P + t * P], xbc[:, 2, ts], xbc[:, 3, ts], start=True, stop=True)
                i.then_inc(full["S1"], 1)
                if not last:
                    project_x("x", "bloop", 0, layer, q)
                pe.wait_ge(ev["ssd_in"], ev_n("ssd_in", layer, g))
                o = fill("S1", f"state{sfx}", layer, q)
                mm(o[:, 0:256], b_tok, xw, start=True, stop=True).then_inc(full["S1"], 1)
                pe.wait_ge(ev["scan_w"], ev_n("scan_w", layer, g))
                o = fill("S0", f"ydiag{sfx}", layer, q)
                for t in range(TOK):
                    for h in range(HG):
                        c = t * 256 + h * HEADDIM
                        i = mm(o[:, c:c + HEADDIM], decay[:, t, h * P:(h + 1) * P],
                               xdt[:, t, h * HEADDIM:(h + 1) * HEADDIM], start=True, stop=True)
                i.then_inc(full["S0"], 1)
                pe.wait_ge(ev["state"], ev_n("state", layer, g))
                o = fill("S1", f"yoff{sfx}", layer, q)
                mm(o[:, 0:256], xbc[:, 3, P:SEQ], st, start=True, stop=True).then_inc(full["S1"], 1)
                if not last:
                    project_bc("bc", "bloop", 2, layer, q)
                pe.wait_ge(ev["yn"], ev_n("yn", layer, g))
                o = fill("S1", f"yT{sfx}", layer, q)
                for k in range(2):
                    for t in range(TOK):
                        i = pe.transpose(o[:, k * SEQ + t * P:k * SEQ + (t + 1) * P],
                                         ysum[:, t, k * P:(k + 1) * P], ident[:, :])
                i.then_inc(full["S1"], 1)
                if not last:
                    project_tok("W0", "z", "bloop", 4, layer, q)
                pe.wait_ge(ev["y_lo"], ev_n("y_lo", layer, gi + (Y_AT["b"] + 1)))
                seg, pos = ("btail", 0) if last else ("bloop", 6)
                for k in range(2):
                    rows(y_hi[:, k, :], y_lo[:, k, :], seg, pos + k, layer, q, stop=last and k == 1)

            def attention(layer, it):
                s = weight("ac", 0, layer, it)
                for c, b in enumerate(("W0", "W1")):
                    o = fill(b, f"qa{c}", layer, it)
                    for e in range(2):
                        h = 2 * c + e
                        for kk in range(2):
                            cs = slice(kk * 512 + h * P, kk * 512 + (h + 1) * P)
                            i = three(o[:, e * SEQ:(e + 1) * SEQ], w_hi[s][:, cs], w_lo[s][:, cs],
                                      c_hi[:, kk, :], c_lo[:, kk, :], kk == 0, kk == 1)
                    i.then_inc(full[b] if c == 0 else used, 1)

                def project_qk(g):
                    b = ("W0", "W1", "W0")[g]
                    o = fill(b, f"qk{g}", layer, it)
                    features(o[:, 0:SEQ], "ac", 1 + 2 * g, layer, it)
                    features(o[:, SEQ:512], "ac", 2 + 2 * g, layer, it)

                project_qk(0)
                pe.wait_ge(ev["qa"], ev_n("qa", layer, it + 1))
                for k, (b, hs) in enumerate((("S0", 0), ("S1", 2))):
                    o = fill(b, f"la{k}", layer, it)
                    for e in range(2):
                        i = mm(o[:, e * SEQ:(e + 1) * SEQ], qa[:, hs + e, P:SEQ], kv_t[:, :],
                               start=True, stop=True)
                    i.then_inc(full[b], 1)
                project_qk(1)
                o = fill("S0", "la2", layer, it)
                for h in range(4):
                    i = mm(o[:, h * P:(h + 1) * P], qa[:, h, 0:P], kv_t[:, 0:P], start=True, stop=True)
                i.then_inc(full["S0"], 1)
                project_qk(2)
                for g in range(CG):
                    pe.wait_ge(ev["qk"], ev_n("qk", layer, it * 3 + (g + 1)))
                    for e, b in enumerate(("S0", "S1")):
                        r = slice(e * C_DIM, (e + 1) * C_DIM)
                        o = fill(b, f"lc{2 * g + e}", layer, it)
                        mm(o[:, 0:P], qk[r, g, 0, 0:P], qk[r, g, 1, 0:P], start=True, stop=True)
                        mm(o[:, P:3 * P], qk[r, g, 0, P:SEQ], qk[r, g, 1, :], start=True, stop=True
                           ).then_inc(full[b], 1)
                project_tok("W1", "ga", "ac", 7, layer, it)
                pe.wait_ge(ev["na"], ev_n("na", layer, it + 1))
                for k in range(3):
                    b = ("S1", "S0", "S1")[k]
                    o = fill(b, f"pa{k}", layer, it)
                    for h in range(4):
                        i = pe.transpose(o[:, h * P:(h + 1) * P], la[:, h, k * P:(k + 1) * P], ident[:, :])
                    i.then_inc(full[b], 1)
                project_tok("W0", "gc", "ac", 9, layer, it)
                pe.wait_ge(ev["pa"], ev_n("pa", layer, it * 3 + 3))
                o = fill("S0", "oa0", layer, it)
                mm(o[:, :], kvn[:, 0, :], pa[:, 0, :], start=True, stop=True).then_inc(full["S0"], 1)
                o = fill("S1", "oa1", layer, it)
                mm(o[:, :], kvn[:, 0, :], pa[:, 1, :], start=True, stop=False)
                mm(o[:, :], kvn[:, 1, :], pa[:, 2, :], start=False, stop=True).then_inc(full["S1"], 1)
                pe.wait_ge(ev["ec"], ev_n("ec", layer, it + 1))
                blocks = [(k, e, g) for k in range(3) for e in range(2) for g in range(CG)]
                for n in range(5):
                    b = ("S0", "S1")[n % 2]
                    o = fill(b, f"pc{n}", layer, it)
                    for i_, (k, e, g) in enumerate(blocks[4 * n:4 * n + 4]):
                        i = pe.transpose(o[:, i_ * P:(i_ + 1) * P], lc[:, e, g, k * P:(k + 1) * P], ident[:, :])
                    i.then_inc(full[b], 1)
                pe.wait_ge(ev["y_lo"], ev_n("y_lo", layer, it + (Y_AT["a"] + 1)))
                for k in range(2):
                    rows(y_hi[:, k, :], y_lo[:, k, :], "ac", 11 + k, layer, it)
                pe.wait_ge(ev["pc"], ev_n("pc", layer, it * 5 + 5))
                o = fill("S1", "oc", layer, it)
                for t in range(TOK):
                    for e in range(2):
                        use = [(n, k, g) for n, (k, ee, g) in enumerate(blocks)
                               if ee == e and (k == 0) == (t == 0)]
                        for m, (n, k, g) in enumerate(use):
                            v = val[:, 1 if k == 2 else 0, g, bass.ds(it * P + e * C_DIM, C_DIM)]
                            c = t * P + e * C_DIM
                            i = mm(o[:, c:c + C_DIM], pc[:, n, :], v, start=m == 0, stop=m == len(use) - 1)
                i.then_inc(full["S1"], 1)
                for k in range(2, 4):
                    rows(y_hi[:, k, :], y_lo[:, k, :], "ac", 11 + k, layer, it)
                pe.wait_ge(ev["nc_"], ev_n("nc_", layer, it + 1))
                o = fill("S0", "ocT", layer, it)
                for t in range(TOK):
                    i = pe.transpose(o[:, t * P:(t + 1) * P], oc_f[:, t, :], ident[:, :])
                i.then_inc(full["S0"], 1)

            pe.sem_inc(used, SLOTS)
            pe.wait_ge(cleared, 3)
            pe.wait_ge(tbl_loaded, 32)
            pe.wait_ge(consts_loaded, 64)
            for v in range(4):
                first, n = (0, A_HEADS) if v == 0 else (A_HEADS + (v - 1) * C_HEADS, C_HEADS)
                mm(acc[v // 2][v % 2][0:n, 0:ROW], tbl[:, first:first + n], oh[:, v, :], start=True, stop=True
                   ).then_inc(tables, 1)
            pe.wait_ge(tables_sb, 4)

            with pe.Fori(0, DEPTH) as layer:
                norm(0, layer)
                ffn("f1", layer)
                norm(1, layer)
                mixer_start(layer)
                acc_zero("b", layer)
                with pe.Fori(1, GROUPS) as g:
                    scan(layer, g, False)
                scan(layer, GROUPS, True)
                acc_zero("a", layer)
                with pe.Fori(0, AC_STEPS) as it:
                    attention(layer, it)
                for t in range(TOK):
                    for h in range(2):
                        i = mm(acc[t][h][:, :], zeros[:, 0:P], zeros[:, :], start=False, stop=True)
                i.then_inc(ev["branch_a"], 1)
                pe.wait_ge(ev["acc_free"], ev_n("acc_free", layer, ACC_USES["c"]))
                pe.wait_ge(ev["y_lo"], ev_n("y_lo", layer, Y_AT["c"] + 1))
                for k in range(4):
                    rows(y_hi[:, k, :], y_lo[:, k, :], "out", k, layer, start=k == 0, stop=k == 3)
                pe.wait_ge(ev["merged"], ev_n("merged", layer, 1))
                turn_rows(gate_b, "mT", layer)
                pe.wait_ge(ev["acc_free"], ev_n("acc_free", layer, ACC_USES["o"]))
                pe.wait_ge(ev["h_lo"], ev_n("h_lo", layer, 12))
                for k in range(8):
                    rows(h_hi[:, k, :], h_lo[:, k, :], "out", 4 + k, layer, start=k == 0, stop=k == 7)
                norm(2, layer)
                ffn("f2", layer)
                norm(3, layer)
                for k, b in enumerate(("W0", "W1", "S0", "S1")):
                    tokens_at(b, "pg", "ple", 2 * k, layer)
                pe.wait_ge(ev["acc_free"], ev_n("acc_free", layer, ACC_USES["ple"]))
                pe.wait_ge(ev["cq_lo"], ev_n("cq_lo", layer, 2))
                for k in range(2):
                    rows(c_hi[:, k, :], c_lo[:, k, :], "ple", 8 + k, layer, start=k == 0, stop=k == 1)

        assert biggest[0] <= 8192 and TOPK == 8 * GROUPS


GAIN_AT = (0, 4, 12, 16)


def look(seg, pos, it, layer):
    if seg == "f1pre" and pos < AHEAD:
        return tile_numbers(seg, pos, it, layer)
    reps, n = SEG_N[seg]
    if reps > 1:
        if pos >= n:
            t0 = SEG_AT[seg] + pos
            every = [t0 + n * r for r in range(reps)]
            assert len({SLOT_OF[t] for t in every}) == 1
            s, step = SLOT_OF[t0], COUNT[t0 + n] - COUNT[t0]
            assert all(COUNT[t] == COUNT[t0] + step * r for r, t in enumerate(every))
            return (layer * TILES + (it * n + t0), s, layer * USES[s] + (it * step + COUNT[t0]),
                    min(BACK[t] for t in every))
        return tile_numbers(seg, pos, it, layer)
    t0 = SEG_AT[seg] + pos
    return layer * TILES + t0, SLOT_OF[t0], layer * USES[SLOT_OF[t0]] + COUNT[t0], BACK[t0]


def _pack_layer(w, i, np_):
    w_in = w["w_in"][i]

    def feat(m, c, n=P):
        return m[:, c:c + n].reshape(KD, P, n).transpose(1, 0, 2).reshape(P, KD * n)

    def tok(m, c, n=256):
        v = feat(m, c, n)
        return [v[:, :TW], v[:, TW:]]

    def row(m, k):
        return m[k * P:(k + 1) * P, :]

    def short(m, c):
        return m[:, c:c + 512].reshape(2, P, 512).transpose(1, 0, 2).reshape(P, TW)

    def ffn(gate, up, down):
        out = []
        for j in range(PAIRS + 1):
            if j < PAIRS:
                for c in (2 * j, 2 * j + 1):
                    out += [feat(gate, c * P), feat(up, c * P)]
            if j > 0:
                out += [row(down, 2 * j - 2), row(down, 2 * j - 1)]
        return out

    tiles = ffn(w["ffn1_gate"][i], w["ffn1_up"][i], w["ffn1_down"][i])
    tiles += tok(w_in, C_CQ)
    second = np_.zeros((D_MODEL, 256), np_.float32)
    second[:, 0:200] = w_in[:, C_CKV:C_CKV + 200]
    second[:, 200:232] = w_in[:, C_DT:C_DT + 32]
    tiles += tok(second, 0)
    for g in range(CG):
        for half in range(2):
            tiles += tok(w_in, C_QKV + g * 1536 + 1024 + half * 256)
    for v in range(4):
        tiles += tok(w_in, C_GB + 256 * v)
    def group(g):
        return [feat(w_in, C_XBC + g * 256), feat(w_in, C_XBC + g * 256 + P),
                feat(w_in, C_XBC + SSM + g * P), feat(w_in, C_XBC + SSM + GROUPS * STATE + g * P)
                ] + tok(w_in, C_Z + g * 256)

    for g in range(GROUPS + 1):
        if g == 0:
            tiles += group(g)[:4] + [short(w["w_iq"][i], 0)] + group(g)[4:]
        elif g < GROUPS:
            tiles += group(g)
        if g > 0:
            tiles += [row(w["w_out_b"][i], 2 * g - 2), row(w["w_out_b"][i], 2 * g - 1)]
    for it in range(AC_STEPS):
        tiles += [short(w["w_uq"][i], 512 * it)]
        for g in range(CG):
            tiles += [feat(w_in, C_QKV + g * 1536 + it * P), feat(w_in, C_QKV + g * 1536 + 512 + it * P)]
        tiles += tok(w_in, C_GA + 256 * it) + tok(w_in, C_GC + 256 * it)
        tiles += [row(w["w_out_a"][i], 4 * it + k) for k in range(4)]
    tiles += [row(w["w_out_c"][i], k) for k in range(4)] + [row(w["w_o"][i], k) for k in range(8)]
    tiles += ffn(w["ffn2_gate"][i], w["ffn2_up"][i], w["ffn2_down"][i])
    for v in range(4):
        tiles += tok(w["w_ple_gate"][i], 256 * v)
    tiles += [row(w["w_ple_proj"][i], k) for k in range(2)]
    assert len(tiles) == TILES, (len(tiles), TILES)
    return tiles


def _pack_params(w, i, np_):
    prm = np_.zeros((P, NPRM), np_.float32)
    for r, name in enumerate(("ffn1_norm", "mix_norm", "ffn2_norm", "ple_norm")):
        prm[:, G_NORM + 8 * r:G_NORM + 8 * r + 8] = w[name][i].reshape(8, P).T
    prm[:, G_CQ:G_CQ + 2] = w["cq_norm"][i].reshape(2, P).T
    prm[:, G_CKV] = w["ckv_norm"][i]
    prm[:, G_EXPA:G_EXPA + 32] = w["a_log"][i][None, :]
    prm[:, G_DTB:G_DTB + 32] = w["dt_bias"][i][None, :]
    for g in range(GROUPS):
        at = G_GRP + g * GRP
        chunks = (g * 256, g * 256 + P, SSM + g * P, SSM + GROUPS * STATE + g * P)
        for c, ch in enumerate(chunks):
            prm[:, at + 4 * c:at + 4 * c + 4] = w["conv_w"][i][:, 0, ch:ch + P].T
            prm[:, at + 16 + c] = w["conv_b"][i][ch:ch + P]
        prm[:, at + 20:at + 22] = w["ssm_norm"][i][g * 256:(g + 1) * 256].reshape(2, P).T
        prm[:, at + 22:at + 26] = w["d_skip"][i][g * HG:(g + 1) * HG][None, :]
    return prm


def _shape_constants(np_):
    j, i = np_.arange(P)[:, None], np_.arange(P)[None, :]
    mask = np_.where(i <= j, 0.0, SCORE_MASK)
    const = np_.concatenate([np_.eye(P), j <= i, j > i, mask, np_.zeros((P, P)), mask],
                            axis=1).astype(np_.float32)
    one_hot = np_.zeros((4, BUCKETS + 1, ROW), np_.float32)
    half = BUCKETS // 2
    for v, (window, step) in enumerate(((SEQ, 1),) + DILATED):
        for m in range(ROW):
            d = SEQ - 1 - m
            if d < 0 or d > window or d % step:
                one_hot[v, BUCKETS, m] = MASKED
                continue
            b = d if d < half else min(BUCKETS - 1, half + int(
                math.log(d / half) / math.log(MAX_DIST / half) * (BUCKETS - half)))
            one_hot[v, b, m] = 1.0
    return const, one_hot


def kernel(**inputs):
    import numpy as _np
    import concourse.bacc as _bacc
    from concourse import mybir as _mybir
    from concourse.bass_utils import run_bass_kernel_spmd as _run

    w = {k: _np.asarray(v) for k, v in inputs.items()}
    weights = _np.empty((DEPTH * TILES, P, TW), _np.float32)
    for i in range(DEPTH):
        for n, tile in enumerate(_pack_layer(w, i, _np)):
            weights[i * TILES + n] = tile
    const, one_hot = _shape_constants(_np)
    arrays = {
        "x_in": _np.ascontiguousarray(w["x"]),
        "weights": weights,
        "params": _np.stack([_pack_params(w, i, _np) for i in range(DEPTH)]),
        "final_gain": _np.ascontiguousarray(w["final_norm"]),
        "ple_in": _np.ascontiguousarray(
            w["p"][:, 0].transpose(0, 2, 1).reshape(DEPTH, 2, P, SEQ).transpose(0, 2, 1, 3)
            .reshape(DEPTH, P, 2 * SEQ)),
        "rel_bias": _np.ascontiguousarray(w["rel_bias"]),
        "constants": const,
        "one_hot": one_hot,
    }
    nc = _bacc.Bacc("TRN2", target_bir_lowering=False, num_devices=1)
    f32 = _mybir.dt.float32
    args = [nc.dram_tensor(n, a.shape, f32, kind="ExternalInput").ap() for n, a in arrays.items()]
    args.append(nc.dram_tensor("out", (1, SEQ, D_MODEL), f32, kind="ExternalOutput").ap())
    trunk(nc, *args)
    r = _run(nc, [arrays], core_ids=[0])
    return r.results[0]["out"]
```

```python
import math
from contextlib import ExitStack

import numpy as np
import concourse.bass as bass
from concourse import mybir

D_MODEL, SEQ, DEPTH, D_FF, PLE_DIM, EPS = 1024, 256, 2, 2816, 256, 1e-6
P = 128
TOK = SEQ // P
KD = D_MODEL // P
A_HEADS, A_DC, A_DCQ = 16, 128, 256
IDX_HEADS, IDX_DIM = 8, 64
TOPK = min(256, SEQ // 4)
GROUPS, HG, HEADDIM, STATE = 8, 4, 64, 128
CG, C_HEADS, C_DIM = 3, 8, 64
DILATED = ((128, 1), (512, 4), (2048, 16))
BUCKETS, MAX_DIST = 32, 2048
HEADS = A_HEADS + CG * C_HEADS
SSM = GROUPS * HG * HEADDIM
TW = 1024
SLOTS = 6
AHEAD = 4
MASKED = -1.0e30
SCORE_MASK, SCORE_TAKEN, SCORE_CUT = -3.0e38, -3.3e38, -3.2e38
DIST = 3 * P - 1
ROW = 384
PAIRS = D_FF // (2 * P)
AC_STEPS = 4
PC_BANKS = ("W1", "W0", "W1", "S0", "S1")

_SIZES = (A_DCQ, A_DC, IDX_DIM, IDX_HEADS, SSM, SSM + 2 * GROUPS * STATE, GROUPS * HG,
          CG * 3 * C_HEADS * C_DIM, D_MODEL, D_MODEL, D_MODEL)
C_CQ, C_CKV, C_KI, C_WI, C_Z, C_XBC, C_DT, C_QKV, C_GA, C_GB, C_GC = (
    int(v) for v in np.concatenate([[0], np.cumsum(_SIZES)[:-1]]))

G_NORM = 0
G_CQ = 32
G_CKV = 34
G_EXPA = 35
G_DTB = 67
G_GRP = 99
GRP = 26
NPRM = G_GRP + GROUPS * GRP

SEGMENTS = [
    ("f1pre", 1, 4), ("f1loop", PAIRS // 2, 12), ("f1tail", 1, 2),
    ("m0", 1, 27), ("bloop", GROUPS - 1, 8), ("btail", 1, 6),
    ("ac", AC_STEPS, 15), ("out", 1, 12),
    ("f2pre", 1, 4), ("f2loop", PAIRS // 2, 12), ("f2tail", 1, 2),
    ("ple", 1, 10),
]


SLOT_PATTERN = {12: (0, 1, 2, 3, 4, 5) * 2, 8: (0, 1, 2, 3, 4, 5, 2, 3),
                15: (0, 1, 2, 3, 4, 0, 1, 2, 5, 3, 0, 1, 2, 4, 5)}


def close_ring(slots, total):
    if len(slots) == total:
        return slots if all(slots[k] not in slots[k - AHEAD + 1:] for k in range(AHEAD - 1)) else None
    recent = list(dict.fromkeys(reversed(slots)))
    for s in recent[::-1]:
        if s not in slots[len(slots) - AHEAD + 1:]:
            found = close_ring(slots + [s], total)
            if found:
                return found
    return None


def plan_tiles():
    seq, seg_at, pattern = [], {}, {}
    owed = []
    for name, reps, n in SEGMENTS:
        lead = owed
        recent = list(dict.fromkeys(s for _, s in reversed(seq)))
        lru = [s for s in range(SLOTS) if s not in recent] + recent[::-1]
        if reps > 1:
            order = lead + [s for s in lru if s not in lead] if lead else lru
            pat = [order[k] for k in SLOT_PATTERN[n]]
            assert len(pat) == n
            pattern[name] = pat
        seg_at[name] = len(seq)
        for r in range(reps):
            for k in range(n):
                if reps > 1:
                    s = pattern[name][k]
                elif k < len(lead):
                    s = lead[k]
                else:
                    recent = list(dict.fromkeys(s for _, s in reversed(seq)))
                    s = ([s for s in range(SLOTS) if s not in recent] + recent[::-1])[0]
                seq.append((name, s))
        owed = pattern[name][:AHEAD] if reps > 1 else owed[n:]
    slots = [s for _, s in seq]
    total = len(slots)
    slots = close_ring(slots[:seg_at[SEGMENTS[-1][0]]], total)
    twice = slots + slots
    back = []
    for t in range(total, 2 * total):
        d = next(d for d in range(1, 2 * total) if twice[t - d] == twice[t])
        assert d >= AHEAD, (seq[t - total][0], t - total, d)
        back.append(min(d, SLOTS))
    count = [slots[:t].count(slots[t]) for t in range(total)]
    return slots, seg_at, back, count, total


SLOT_OF, SEG_AT, BACK, COUNT, TILES = plan_tiles()
USES = [SLOT_OF.count(s) for s in range(SLOTS)]
SEG_N = {name: (reps, n) for name, reps, n in SEGMENTS}


def tile_numbers(seg, pos, it, layer):
    reps, n = SEG_N[seg]
    t0 = SEG_AT[seg] + pos
    if reps == 1:
        return layer * TILES + t0, SLOT_OF[t0], layer * USES[SLOT_OF[t0]] + COUNT[t0], BACK[t0]
    every = [t0 + n * r for r in range(reps)]
    assert len({SLOT_OF[t] for t in every}) == 1
    s = SLOT_OF[t0]
    step = COUNT[t0 + n] - COUNT[t0]
    assert all(COUNT[t] == COUNT[t0] + step * r for r, t in enumerate(every))
    return (layer * TILES + (it * n + t0), s, layer * USES[s] + (it * step + COUNT[t0]),
            min(BACK[t] for t in every))


def _norm(r):
    return (1, [(b, f"norm{r}") for b in ("W0", "W1", "S0", "S1")])


def _ffn(f):
    return [(PAIRS, [("W0", f"{f}even"), ("W1", f"{f}odd")])]


FILL_ORDER = (
    [_norm(0)] + _ffn("f1") + [_norm(1)]
    + [(1, [("W0", "small0"), ("W1", "small1")]),
       (3, [("W0", "v_even"), ("W1", "v_odd")]),
       (1, [("S0", "cqT"), ("S1", "kvT"), ("S0", "cum")]),
       (1, [("S0", "qi0"), ("S1", "qi1")]),
       (1, [("W0", "x_first"), ("W1", "bc_first"), ("W0", "z_first"), ("W1", "gb0"), ("W0", "gb1")]),
       (2, [("S0", "sc1_even"), ("S1", "sc1_odd")]),
       (1, [("S0", "sc0_even"), ("S1", "sc0_odd")]),
       (GROUPS - 1, [("W0", "seg0"), ("W1", "seg1"), ("S0", "xT"), ("S1", "bcb"), ("W0", "x"),
                     ("S1", "state"), ("S0", "ydiag"), ("S1", "yoff"), ("W1", "bc"),
                     ("S1", "yT"), ("W0", "z")]),
       (1, [("W0", "seg0_last"), ("W1", "seg1_last"), ("S0", "xT_last"), ("S1", "bcb_last"),
            ("W0", "gb2"), ("W1", "gb3"),
            ("S1", "state_last"), ("S0", "ydiag_last"), ("S1", "yoff_last"), ("S1", "yT_last")]),
       (AC_STEPS, [("W0", "qa0"), ("W1", "qa1"), ("W0", "qk0"), ("S0", "la0"), ("S1", "la1"),
                   ("W1", "qk1"), ("S0", "la2"), ("W0", "qk2"),
                   ("S0", "lc0"), ("S1", "lc1"), ("S0", "lc2"), ("S1", "lc3"), ("S0", "lc4"),
                   ("S1", "lc5"), ("W1", "ga"), ("W0", "pa0"), ("S0", "pa1"), ("S1", "pa2"),
                   ("W0", "gc"), ("W1", "pc0"), ("S0", "oa0"), ("S1", "oa1"),
                   ("W0", "pc1"), ("W1", "pc2"), ("S0", "pc3"), ("S1", "pc4"),
                   ("S1", "oc"), ("S0", "ocT")]),
       (1, [("W0", "branch_c"), ("W1", "branch_c"), ("S0", "branch_c"), ("S1", "branch_c")]),
       (1, [("W0", "mT"), ("W1", "mT"), ("S0", "mT"), ("S1", "mT")])]
    + [_norm(2)] + _ffn("f2") + [_norm(3)]
    + [(1, [("W0", "pg"), ("W1", "pg"), ("S0", "pg"), ("S1", "pg")])]
)


BY_TILES = {"norm0", "norm1", "norm2", "norm3", "qi1", "qa1", "f1even", "f1odd", "f2even", "f2odd", "small0", "small1", "v_even", "v_odd", "gb0", "gb1", "gb2", "gb3", "branch_c",
            "x_first", "bc_first", "z_first", "x", "bc", "z", "qk0", "qk1", "qk2", "ga", "gc", "pg"}


BY_SPLIT = {"pg", "norm0", "norm1", "norm2", "norm3", "mT", "yT", "yT_last"}


def plan_fills(without):
    at, step, total = {}, {}, dict.fromkeys(("W0", "W1", "S0", "S1"), 0)
    for reps, fills in FILL_ORDER:
        per = {b: sum(1 for x, name in fills if x == b and name not in without) for b in total}
        seen = dict.fromkeys(total, 0)
        for b, name in fills:
            at[b, name] = total[b] + seen[b]
            step[b, name] = per[b]
            seen[b] += name not in without
        for b in total:
            total[b] += per[b] * reps
    return at, step, total


FREE_PLAN, FULL_PLAN = plan_fills(BY_SPLIT), plan_fills(BY_TILES)

ACC_USES = {"f1": 0, "b": 1, "a": 2, "o": 3, "f2": 4, "ple": 5}
Y_AT = {"f1": 0, "b": PAIRS, "a": PAIRS + GROUPS, "f2": PAIRS + GROUPS + AC_STEPS}
Y_USES = 2 * PAIRS + GROUPS + AC_STEPS
Y_SRC_AT = {"f1": 0, "f2": PAIRS}

PER_LAYER = dict(
    x_done=8, squares=4, rstd=4, diag=4, rstd_row=4, normed=16, h_hi=20, h_lo=20,
    ffn_tanh=4 * PAIRS, y_src=2 * PAIRS, y_hi=Y_USES, y_lo=Y_USES, 
    acc_free=6,
    small=2, prep_squares=1, prep_rstd=1, prep_n=1, cq_gained=1, cq_hi=2, cq_lo=2, ki=1,
    kv=1, dt_in=1, dt_ln=1, da=1, ecum=1, wlast=1, v_sb=6, gates=8 + 4 + 4 + 4,
    qi=2, relu=6, weighted=6, chosen=1,
    dau=GROUPS, decay=2 * GROUPS, ssd_in=GROUPS, scan_w=GROUPS, state=GROUPS, y_sum=GROUPS,
    y_squares=GROUPS, y_rstd=GROUPS, yn=GROUPS, pre_x=GROUPS, pre_bc=GROUPS, conv=2 * GROUPS,
    conv_tanh=2 * GROUPS, xbc=GROUPS, z_tanh=GROUPS, zz=GROUPS, taps=GROUPS,
    qa=AC_STEPS, qk=3 * AC_STEPS, la=AC_STEPS, ea=AC_STEPS, na=AC_STEPS, pa=3 * AC_STEPS,
    lc=AC_STEPS, ec=AC_STEPS, nc_=AC_STEPS, oc_lo=AC_STEPS, pc=5 * AC_STEPS, oc=AC_STEPS,
    branch_a=1, merged=2,
)


SEEDED = ("x_done", "y_src", "acc_free", "conv", "y_sum", "pc", "lc")


def trunk(nc, x_in, weights, params, final_gain, ple_in, rel_bias, constants, one_hot, out):
    f32, f32r, bf16 = mybir.dt.float32, mybir.dt.float32r, mybir.dt.bfloat16
    ACT, ALU, AX = mybir.ActivationFunctionType, mybir.AluOpType, mybir.AxisListType
    MUL, ADD, SUB, MAX = ALU.mult, ALU.add, ALU.subtract, ALU.max

    with ExitStack() as ctx:
        def sb(name, shape, dt=f32):
            return ctx.enter_context(nc.sbuf_tensor(name, shape, dt))

        def sem(name):
            return ctx.enter_context(nc.semaphore(name))

        raw = [sb(f"raw{s}", [P, TW]) for s in range(SLOTS)]
        w_hi = [sb(f"w_hi{s}", [P, TW], f32r) for s in range(SLOTS)]
        w_lo = [sb(f"w_lo{s}", [P, TW], f32r) for s in range(SLOTS)]
        x = sb("x", [P, TOK, D_MODEL])
        h_hi = sb("h_hi", [P, KD, SEQ], f32r)
        h_lo = sb("h_lo", [P, KD, SEQ], f32r)
        y_hi = sb("y_hi", [P, 4, SEQ], f32r)
        y_lo = sb("y_lo", [P, 4, SEQ], f32r)
        c_hi = sb("c_hi", [P, 2, SEQ], f32r)
        c_lo = sb("c_lo", [P, 2, SEQ], f32r)
        ident = sb("ident", [P, P])
        upto = sb("upto", [P, P])
        after = sb("after", [P, P])
        causal = sb("causal", [P, 3 * P])
        zeros = sb("zeros", [P, 512], bf16)
        ones = sb("ones", [P, P])
        prm = sb("prm", [P, NPRM])
        minus_half = sb("minus_half", [P, 4])
        val = sb("val", [P, TOK, CG, 512])
        kvn = sb("kvn", [P, TOK, A_DC])
        kv_t = sb("kv_t", [P, SEQ])
        ki_t = sb("ki_t", [P, SEQ])
        score = sb("score", [P, 3 * P])
        top8 = sb("top8", [P, 2, 8])
        wix = sb("wix", [P, TOK, IDX_HEADS])
        dts = sb("dts", [P, TOK, 32])
        da = sb("da", [P, TOK, 32])
        wl = sb("wl", [P, 32])
        ecum = sb("ecum", [P, 32])
        gate_b = sb("gate_b", [P, TOK, D_MODEL])
        gate_a = sb("gate_a", [P, TOK, D_MODEL])
        gate_c = sb("gate_c", [P, TOK, D_MODEL])
        yc_hi = sb("yc_hi", [P, AC_STEPS, SEQ], f32r)
        yc_lo = sb("yc_lo", [P, AC_STEPS, SEQ], f32r)
        bias = sb("bias", [P, 10, SEQ])
        stat = sb("stat", [P, 64])
        taps = sb("taps", [P, 20])
        arena = sb("arena", [P, 8192])
        biggest = [0]

        def part(at, shape, rows=P):
            n = int(np.prod(shape))
            biggest[0] = max(biggest[0], at + n)
            v = arena[0:rows, at:at + n]
            if len(shape) == 2:
                return v.rearrange("p (a b) -> p a b", a=shape[0])
            if len(shape) == 3:
                return v.rearrange("p (a b c) -> p a b c", a=shape[0], b=shape[1])
            return v

        diag = part(0, (TOK, P))
        rstd_row = part(256, (SEQ,))
        normed = part(2048, (KD, SEQ))
        junk = part(4096, (1024,))
        act_f = part(5120, (2, SEQ))
        ffn_t = part(5632, (2, SEQ))
        small = part(0, (TOK, 512))
        cqn = part(1024, (TOK, A_DCQ))
        cqf = part(1536, (512,))
        dt_a = part(2048, (2, 64))
        relu = part(2304, (2, 512))
        qi = part(3328, (IDX_HEADS // 2, SEQ))
        ki2 = part(2304, (TOK, P))
        sq_m0 = part(5376, (256,))
        pre = part(5636, (4, 3 + SEQ))
        xbc = part(6672, (4, SEQ))
        conv_t = part(1024, (4, SEQ))
        dau = part(0, (TOK, 512))
        decay = part(1024, (TOK, 512))
        xdt = part(2048, (TOK, 256))
        xd = part(2560, (TOK, 256))
        xw = part(3072, (256,))
        b_tok = part(3328, (P,))
        cbm = part(3456, (TOK, P))
        zz = part(5120, (TOK, 256))
        ysum = part(3712, (TOK, 256))
        st = part(4224, (256,))
        yoffs = part(4480, (256,))
        sq_b = part(4736, (256,))
        qa = part(0, (4, SEQ))
        la = part(1024, (4, 3 * P))
        pa = part(2560, (3, 512))
        pc = part(1024, (18, P))
        qk = part(4096, (CG, 2, SEQ))
        lc = part(5632, (2, CG, 3 * P))
        oc_f = part(7936, (TOK, P))
        pg = part(0, (TOK, D_MODEL))
        pin = part(6144, (512,))
        fgain = part(2048, (D_MODEL,))
        oh = part(512, (4, ROW), rows=33)
        tbl = part(0, (HEADS,), rows=33)
        rb = part(6656, (4, ROW), rows=16)

        bank = {b: ctx.enter_context(nc.psum_tensor(f"bank_{b}", [P, 512], f32))
                for b in ("W0", "W1", "S0", "S1")}
        acc = [[ctx.enter_context(nc.psum_tensor(f"acc{t}{h}", [P, 512], f32)) for h in range(2)]
               for t in range(TOK)]
        W0, W1, S0, S1 = (bank[b] for b in ("W0", "W1", "S0", "S1"))
        arrived = [sem(f"arrived{s}") for s in range(SLOTS)]
        hi_done, lo_done, used = sem("hi_done"), sem("lo_done"), sem("used")
        full = {b: sem(f"full_{b}") for b in bank}
        free = {b: sem(f"free_{b}") for b in bank}
        ev = {n: sem(n) for n in PER_LAYER}
        x_loaded, consts_loaded, prm_loaded = sem("x_loaded"), sem("consts_loaded"), sem("prm_loaded")
        tbl_loaded, tables, tables_sb, tables_out = sem("tbl_loaded"), sem("tables"), sem("tables_sb"), sem("tables_out")
        bias_loaded, ple_loaded, fgain_loaded = sem("bias_loaded"), sem("ple_loaded"), sem("fgain_loaded")
        cleared, out_done, prm_halved, final = sem("cleared"), sem("out_done"), sem("prm_halved"), sem("final")

        scratch = nc.dram_tensor("distance_tables", (HEADS, ROW), f32, kind="Internal").ap()
        blocks = nc.dram_tensor("distance_blocks", (HEADS, P, SEQ), f32, kind="Internal").ap()
        blocks_out, pool_steps = sem("blocks_out"), sem("pool_steps")

        def ev_n(name, layer, n):
            return layer * PER_LAYER[name] + (n + (name in SEEDED))

        def free_n(b, name, layer, it=0):
            at, step, total = FREE_PLAN
            return layer * total[b] + (it * step[b, name] + (at[b, name] + 1))

        def fill_n(b, name, layer, it=0):
            at, step, total = FULL_PLAN
            return layer * total[b] + (it * step[b, name] + (at[b, name] + 1))

        def done(seg, pos, layer, it=0):
            return layer * TILES + (it * SEG_N[seg][1] + (SEG_AT[seg] + pos + 1 + SLOTS))

        def indexer_fill(k):
            if k < 4:
                first = 4 * (k // 2) + k % 2
                return (first, first + 2), SEQ, P, 1
            return tuple(range(k % 2, IDX_HEADS, 2)), P, 0, 0

        block = ctx.enter_context(nc.Block())

        @block.sync
        def _(sp):
            sp.dma_start(x[:, :, :], x_in.rearrange("o (t p) d -> p (o t) d", p=P)).then_inc(x_loaded, 16)
            sp.dma_start(ident[:, :], constants[:, 0:P]).then_inc(consts_loaded, 16)
            sp.dma_start(upto[:, :], constants[:, P:2 * P]).then_inc(consts_loaded, 16)
            sp.dma_start(after[:, :], constants[:, 2 * P:3 * P]).then_inc(consts_loaded, 16)
            sp.dma_start(causal[:, :], constants[:, 3 * P:6 * P]).then_inc(consts_loaded, 16)

            def stream(seg, layer, it=0):
                for pos in range(SEG_N[seg][1]):
                    t, s, count, back = tile_numbers(seg, pos, it, layer)
                    sp.wait_ge(lo_done, t - back + 1 + SLOTS)
                    sp.dma_start(raw[s][:, :], weights[bass.ts(t, 1), :, :].rearrange("o p n -> (o p) n")
                                 ).then_inc(arrived[s], 16)

            with sp.Fori(0, DEPTH) as layer:
                stream("f1pre", layer)
                for seg, reps, _ in SEGMENTS[1:]:
                    if reps > 1:
                        with sp.Fori(0, reps) as it:
                            stream(seg, layer, it)
                    else:
                        stream(seg, layer)

        @block.gpsimd
        def _(pool):
            pool.memset(minus_half[:, :], -0.5).then_inc(cleared, 1)
            pool.drain()
            pool.drain()
            pool.memset(tbl[32:33, :], 1.0).then_inc(cleared, 1)
            pool.dma_start(tbl[0:32, :], rel_bias).then_inc(tbl_loaded, 16)
            pool.dma_start(oh, one_hot.rearrange("v r d -> r v d")).then_inc(tbl_loaded, 16)
            pool.dma_start(prm[:, :], params[0, :, :]).then_inc(prm_loaded, 16)

            def row_power(mean, n_cols, scales, first):
                at = first
                for cols, scale in scales:
                    pool.tensor_scalar(stat[:, at:at + cols], stat[:, at:at + cols], scale, EPS, MUL, ADD)
                    at += cols
                    pool.drain()
                return pool.tensor_tensor(stat[:, first:first + n_cols], stat[:, first:first + n_cols],
                                          minus_half[:, 0:n_cols], ALU.pow)

            def settled():
                pool.sem_inc(pool_steps, 1)

            def norm(r, layer):
                pool.wait_ge(ev["squares"], ev_n("squares", layer, r + 1))
                settled()
                row_power(None, TOK, [(TOK, 1.0 / D_MODEL)], 0).then_inc(ev["rstd"], 1)
                pool.drain()

            def load_bias(layer, it):
                pool.wait_ge(blocks_out, 64)
                pool.wait_ge(ev["lc"], ev_n("lc", layer, it))
                settled()
                pool.dma_start(bias[:, 0:4, :], blocks[bass.ds(it * 4, 4), :, :].rearrange("h p s -> p h s")
                               ).then_inc(bias_loaded, 16)
                for g in range(CG):
                    heads = blocks[bass.ds(it * 2 + (A_HEADS + g * C_HEADS), 2), :, :]
                    pool.dma_start(bias[:, 4 + 2 * g:6 + 2 * g, :], heads.rearrange("h p s -> p h s")
                                   ).then_inc(bias_loaded, 16)

            def cum_steps(layer, g):
                for t in range(TOK):
                    pool.drain()
                    pool.tensor_tensor(
                        dau[:, t, :].rearrange("p (h i) -> p h i", h=HG),
                        upto[:, :].unsqueeze(1).broadcast_to([P, HG, P]),
                        da[:, t, bass.ts(g, HG)].unsqueeze(2).broadcast_to([P, HG, P]), MUL)
                pool.drain().then_inc(ev["dau"], 1)

            def distance_tables():
                pool.wait_ge(tables_sb, 4)
                for v in range(4):
                    first, n = (0, A_HEADS) if v == 0 else (A_HEADS + (v - 1) * C_HEADS, C_HEADS)
                    pool.dma_start(scratch[first:first + n, :], rb[0:n, v, :]).then_inc(tables_out, 16)
                pool.wait_ge(tables_out, 64)
                for n in range(0, HEADS, HEADS // 4):
                    skewed = bass.AP(tensor=scratch.tensor, offset=n * ROW + (P - 1),
                                     ap=[[ROW, HEADS // 4], [-1, P], [1, SEQ]])
                    pool.dma_start(blocks[n:n + HEADS // 4, :, :], skewed).then_inc(blocks_out, 16)

            pool.drain()
            norm(0, 0)
            distance_tables()
            with pool.Fori(0, DEPTH) as layer:
                norm(1, layer)
                pool.wait_ge(ev["prep_squares"], ev_n("prep_squares", layer, 1))
                settled()
                row_power(None, 4, [(2, 1.0 / A_DCQ), (2, 1.0 / A_DC)], 4).then_inc(ev["prep_rstd"], 1)
                pool.wait_ge(full["S1"], fill_n("S1", "kvT", layer))
                pool.wait_ge(ev["da"], ev_n("da", layer, 1))
                settled()

                def group_taps(g):
                    pool.wait_ge(ev["conv"], ev_n("conv", layer, 2 * g))
                    settled()
                    pool.tensor_copy(taps[:, :], prm[:, bass.ds(g * GRP + G_GRP, 20)])
                    pool.drain().then_inc(ev["taps"], 1)

                group_taps(0)
                cum_steps(layer, 0)

                def scan(g, last):
                    if not last:
                        group_taps(g)
                    pool.wait_ge(ev["y_squares"], ev_n("y_squares", layer, g))
                    settled()
                    row_power(None, TOK, [(TOK, 1.0 / 256)], 8).then_inc(ev["y_rstd"], 1)
                    if not last:
                        pool.wait_ge(full["W1"], fill_n("W1", "seg1", layer, g - 1))
                        settled()
                        cum_steps(layer, g)

                with pool.Fori(1, GROUPS) as g:
                    scan(g, False)
                scan(GROUPS, True)
                with pool.Fori(0, AC_STEPS) as it:
                    load_bias(layer, it)
                norm(2, layer)
                pool.dma_start(pin, ple_in[bass.ts(layer, 1), :, :].rearrange("o p n -> (o p) n")
                               ).then_inc(ple_loaded, 16)
                norm(3, layer)
                pool.wait_ge(ev["h_lo"], ev_n("h_lo", layer, 20))
                settled()
                pool.dma_start(prm[:, :], params[bass.ds(layer + 1, 1), :, :].rearrange("o p n -> (o p) n")
                               ).then_inc(prm_loaded, 16)
                norm(0, layer + 1)
            pool.wait_ge(ev["x_done"], 8 * DEPTH + 1)
            pool.dma_start(fgain, final_gain.partition_broadcast(P)).then_inc(fgain_loaded, 16)
            pool.wait_ge(final, TOK)
            for t in range(TOK):
                pool.dma_start(out[0, t * P:(t + 1) * P, :], x[:, t, :]).then_inc(out_done, 16)
            pool.wait_ge(out_done, 16 * TOK)
            pool.wait_ge(prm_loaded, 16 * (DEPTH + 1))

        @block.scalar
        def _(act):
            A = act.activation
            act.preload_act_table_set("exp_and_others")

            def w_split(seg, pos, layer, it=0):
                t, s, count, back = look(seg, pos + AHEAD, it, layer)
                act.wait_ge(arrived[s], count * 16 + 16)
                act.wait_ge(used, t - back + 1 + SLOTS)
                A(w_hi[s][:, :], raw[s][:, :], ACT.Copy).then_inc(hi_done, 1)

            def norm(r, layer):
                for t in range(TOK):
                    act.drain()
                    act.wait_ge(ev["x_done"], ev_n("x_done", layer, 2 * (r - 1) + t + 1 if r else 0))
                    act.wait_ge(x_loaded, 16)
                    i = A(junk, x[:, t, :], ACT.Square, accum_out=stat[:, t:t + 1])
                i.then_inc(ev["squares"], 1)

            def norm_hi(r, layer):
                for b in range(4):
                    act.wait_ge(ev["normed"], ev_n("normed", layer, 4 * r + b + 1))
                    A(h_hi[:, 2 * b:2 * b + 2, :], normed[:, 2 * b:2 * b + 2, :], ACT.Copy
                      ).then_inc(ev["h_hi"], 1)

            def y_split(f, layer, j, c0):
                act.wait_ge(ev["y_src"], ev_n("y_src", layer, j + Y_SRC_AT[f] + 1))
                A(y_hi[:, c0:c0 + 2, :], act_f, ACT.Copy).then_inc(ev["y_hi"], 1)

            def ffn(f, layer):
                def chunk(j, c, seg, pos, it=0):
                    b = ("W0", "W1")[c]
                    act.wait_ge(used, done(seg, pos, layer, it))
                    act.wait_ge(ev["y_src"], ev_n("y_src", layer, j + Y_SRC_AT[f]))
                    A(ffn_t[:, c, :], bank[b][:, 0:SEQ], ACT.Tanh, scale=0.5).then_inc(ev["ffn_tanh"], 1)

                w_split(f + "pre", 0, layer)
                chunk(0, 0, f + "pre", 1)
                w_split(f + "pre", 1, layer)
                w_split(f + "pre", 2, layer)
                chunk(0, 1, f + "pre", 3)
                w_split(f + "pre", 3, layer)
                y_split(f, layer, 0, 0)
                with act.Fori(0, PAIRS // 2) as i:
                    for u in range(2):
                        j, at = i * 2 + (1 + u), 6 * u
                        w_split(f + "loop", at, layer, i)
                        chunk(j, 0, f + "loop", at + 1, i)
                        w_split(f + "loop", at + 1, layer, i)
                        w_split(f + "loop", at + 2, layer, i)
                        chunk(j, 1, f + "loop", at + 3, i)
                        if u == 0:
                            act.wait_ge(used, done(f + "loop", 11, layer, i - 1))
                        else:
                            act.wait_ge(used, done(f + "loop", 5, layer, i))
                        y_split(f, layer, j, 2 - 2 * u)
                        for k in (3, 4, 5):
                            w_split(f + "loop", at + k, layer, i)
                for k in range(2):
                    w_split(f + "tail", k, layer)

            def conv_evac(layer, g, c0, name, it):
                b, pre_done = (W0, ev["pre_x"]) if c0 == 0 else (W1, ev["pre_bc"])
                if c0 == 0:
                    act.wait_ge(ev["conv"], ev_n("conv", layer, 2 * g))
                    act.wait_ge(ev["taps"], ev_n("taps", layer, g + 1))
                act.wait_ge(used, done(*name, layer, it))
                A(pre[:, c0:c0 + 2, 3:3 + SEQ], b[:, :].rearrange("p (c t) -> p c t", c=2), ACT.Copy)
                for c in range(c0, c0 + 2):
                    A(xbc[:, c, :], b[:, (c - c0) * SEQ:(c - c0 + 1) * SEQ], ACT.Identity,
                      scale=taps[:, 4 * c + 3:4 * c + 4], bias=taps[:, 16 + c:17 + c])
                act.drain().then_inc(pre_done, 1)
                act.sem_inc(free["W0" if c0 == 0 else "W1"], 1)

            def conv_tanh(layer, g, c0):
                act.wait_ge(ev["conv"], ev_n("conv", layer, 2 * g + (c0 // 2 + 1)))
                A(conv_t[:, c0:c0 + 2, :], xbc[:, c0:c0 + 2, :], ACT.Tanh).then_inc(ev["conv_tanh"], 1)

            def gate_b_tanh(layer, v, b, seg, pos):
                act.wait_ge(used, done(seg, pos, layer))
                A(gate_b[:, :, v * 256:v * 256 + 256], bank[b][:, :].rearrange("p (t c) -> p t c", t=TOK),
                  ACT.Tanh, scale=0.5).then_inc(free[b], 1)

            def z_tanh(layer, g, name, it):
                act.wait_ge(used, done(*name, layer, it))
                act.wait_ge(ev["y_sum"], ev_n("y_sum", layer, g))
                A(zz, W0[:, :].rearrange("p (t c) -> p t c", t=TOK), ACT.Tanh, scale=0.5
                  ).then_inc(ev["z_tanh"], 1)

            def mixer_start(layer):
                split = iter(range(27))

                def w(n):
                    for _ in range(n):
                        w_split("m0", next(split), layer)
                w(2)
                act.wait_ge(used, done("m0", 1, layer))
                A(small[:, :, 0:256], W0[:, :].rearrange("p (t c) -> p t c", t=TOK), ACT.Copy
                  ).then_inc(free["W0"], 1)
                w(2)
                act.wait_ge(used, done("m0", 3, layer))
                A(small[:, :, 256:512], W1[:, :].rearrange("p (t c) -> p t c", t=TOK), ACT.Copy
                  ).then_inc(free["W1"], 1)
                act.drain().then_inc(ev["small"], 2)
                for t in range(TOK):
                    A(sq_m0, small[:, t, 0:256], ACT.Square, accum_out=stat[:, 4 + t:5 + t])
                    act.drain()
                for t in range(TOK):
                    A(sq_m0[:, 0:P], small[:, t, 256:384], ACT.Square, accum_out=stat[:, 6 + t:7 + t])
                    act.drain()
                act.drain().then_inc(ev["prep_squares"], 1)
                act.wait_ge(ev["dt_in"], ev_n("dt_in", layer, 1))
                A(prm[:, G_EXPA:G_EXPA + 32], prm[:, G_EXPA:G_EXPA + 32], ACT.Exp)
                A(dt_a[:, 1, :], dt_a[:, 1, :], ACT.Exp, scale=-1.0)
                act.drain()
                A(dt_a[:, 1, :], dt_a[:, 1, :], ACT.Ln, bias=1.0).then_inc(ev["dt_ln"], 1)
                act.preload_act_table_set("exp_and_others")
                for u in range(6):
                    b = ("W0", "W1")[u % 2]
                    w(2)
                    act.wait_ge(used, done("m0", 5 + 2 * u, layer))
                    A(val[:, :, u // 2, (u % 2) * 256:(u % 2) * 256 + 256],
                      bank[b][:, :].rearrange("p (t c) -> p t c", t=TOK), ACT.Copy).then_inc(free[b], 1)
                act.drain().then_inc(ev["v_sb"], 6)
                act.wait_ge(ev["cq_gained"], ev_n("cq_gained", layer, 1))
                act.wait_ge(ev["x_done"], ev_n("x_done", layer, 2))
                A(c_hi[:, :, :], cqf.rearrange("p (k t) -> p k t", k=2), ACT.Copy).then_inc(ev["cq_hi"], 1)
                act.wait_ge(full["S0"], fill_n("S0", "cum", layer))
                A(ecum[:, :], S0[:, 0:32], ACT.Exp)
                A(wl[:, :], S0[:, 32:64], ACT.Exp).then_inc(free["S0"], 1)
                act.drain().then_inc(ev["ecum"], 1)
                w(2)
                conv_evac(layer, 0, 0, ("m0", 17), 0)
                w(2)
                conv_evac(layer, 0, 2, ("m0", 19), 0)
                act.wait_ge(full["S0"], fill_n("S0", "qi0", layer))
                A(qi[:, 0:2, :], S0[:, :].rearrange("p (h t) -> p h t", h=2), ACT.Copy).then_inc(free["S0"], 1)
                act.wait_ge(used, done("m0", 20, layer))
                A(qi[:, 2:4, :], S1[:, :].rearrange("p (h t) -> p h t", h=2), ACT.Copy).then_inc(free["S1"], 1)
                act.drain().then_inc(ev["qi"], 2)
                w(1)
                conv_tanh(layer, 0, 0)
                conv_tanh(layer, 0, 2)
                w(2)
                z_tanh(layer, 0, ("m0", 22), 0)
                for k in range(6):
                    b, name = (("S0", "sc1_even"), ("S1", "sc1_odd"))[k % 2] if k < 4 else \
                        (("S0", "sc0_even"), ("S1", "sc0_odd"))[k % 2]
                    act.wait_ge(full[b], fill_n(b, name, layer, k // 2 if k < 4 else 0))
                    if k >= 2:
                        act.wait_ge(ev["weighted"], ev_n("weighted", layer, k - 1))
                    A(relu[:, k % 2, :], bank[b][:, :], ACT.Relu).then_inc(free[b], 1)
                    act.drain().then_inc(ev["relu"], 1)
                    if k == 1:
                        w(2)
                    if k in (1, 3):
                        gate_b_tanh(layer, k // 2, ("W1", "W0")[k // 2], "m0", 24 + 2 * (k // 2))

            def scan(layer, g, last):
                sfx = "_last" if last else ""
                q = 0 if last else g - 1
                for t, b in enumerate(("W0", "W1")):
                    act.wait_ge(full[b], fill_n(b, f"seg{t}{sfx}", layer, q))
                    if t == 0:
                        act.wait_ge(ev["xbc"], ev_n("xbc", layer, g))
                    A(decay[:, t, :], bank[b][:, :], ACT.Exp).then_inc(free[b], 1)
                    act.drain().then_inc(ev["decay"], 1)
                for k in (-2, -1):
                    w_split("btail" if last else "bloop", k, layer, q)
                if not last:
                    conv_evac(layer, g, 0, ("bloop", 1), q)
                act.wait_ge(full["S1"], fill_n("S1", f"state{sfx}", layer, q))
                A(st, S1[:, 0:256], ACT.Copy).then_inc(free["S1"], 1)
                act.drain().then_inc(ev["state"], 1)
                for k in (0, 1):
                    w_split("btail" if last else "bloop", k, layer, q)
                if last:
                    gate_b_tanh(layer, 2, "W0", "btail", 1)
                act.wait_ge(ev["y_sum"], ev_n("y_sum", layer, g))
                for t in range(TOK):
                    A(sq_b, ysum[:, t, :], ACT.Square, accum_out=stat[:, 8 + t:9 + t])
                    act.drain()
                act.drain().then_inc(ev["y_squares"], 1)
                w_split("btail" if last else "bloop", 2, layer, q)
                act.wait_ge(ev["y_rstd"], ev_n("y_rstd", layer, g))
                for t in range(TOK):
                    A(ysum[:, t, :], ysum[:, t, :], ACT.Copy, scale=stat[:, 8 + t:9 + t])
                act.drain().then_inc(ev["yn"], 1)
                if not last:
                    conv_evac(layer, g, 2, ("bloop", 3), q)
                else:
                    gate_b_tanh(layer, 3, "W1", "btail", 3)
                    act.drain().then_inc(ev["gates"], 8)
                act.wait_ge(used, done("bloop", 7, layer, g - 2))
                act.wait_ge(full["S1"], fill_n("S1", f"yT{sfx}", layer, q))
                for k in range(2):
                    i = A(y_hi[:, k, :], S1[:, k * SEQ:(k + 1) * SEQ], ACT.Copy,
                          scale=prm[:, bass.ds((g - 1) * GRP + (G_GRP + 20 + k), 1)])
                i.then_inc(ev["y_hi"], 1)
                w_split("btail" if last else "bloop", 3, layer, q)
                if not last:
                    conv_tanh(layer, g, 0)
                w_split("btail" if last else "bloop", 4, layer, q)
                if not last:
                    conv_tanh(layer, g, 2)
                    z_tanh(layer, g, ("bloop", 5), q)
                w_split("btail" if last else "bloop", 5, layer, q)

            def attention(layer, it):
                def w(*ps):
                    for p in ps:
                        w_split("ac", p, layer, it)
                act.wait_ge(full["W0"], fill_n("W0", "qa0", layer, it))
                A(qa[:, 0:2, :], W0[:, :].rearrange("p (h t) -> p h t", h=2), ACT.Copy).then_inc(free["W0"], 1)
                act.wait_ge(used, done("ac", 0, layer, it))
                A(qa[:, 2:4, :], W1[:, :].rearrange("p (h t) -> p h t", h=2), ACT.Copy).then_inc(free["W1"], 1)
                act.drain().then_inc(ev["qa"], 1)
                w(0, 1, 2)

                def evacuate_qk(g, b):
                    act.wait_ge(used, done("ac", 2 + 2 * g, layer, it))
                    A(qk[:, g, :, :], bank[b][:, :].rearrange("p (a t) -> p a t", a=2), ACT.Copy
                      ).then_inc(free[b], 1)
                    act.drain().then_inc(ev["qk"], 1)

                evacuate_qk(0, "W0")
                w(3, 4)
                evacuate_qk(1, "W1")
                w(5, 6)
                evacuate_qk(2, "W0")
                w(7)
                act.wait_ge(ev["la"], ev_n("la", layer, it + 1))
                for h in range(4):
                    for t in range(TOK):
                        s = la[:, h, 0:P] if t == 0 else la[:, h, P:3 * P]
                        A(s, s, ACT.Exp, bias=stat[:, 16 + 4 * t + h:17 + 4 * t + h],
                          accum_out=stat[:, 24 + 4 * t + h:25 + 4 * t + h])
                act.drain().then_inc(ev["ea"], 1)
                w(8)
                for k in range(3):
                    b = ("W0", "S0", "S1")[k]
                    act.wait_ge(full[b], fill_n(b, f"pa{k}", layer, it))
                    A(pa[:, k, :], bank[b][:, :], ACT.Copy).then_inc(free[b], 1)
                    act.drain().then_inc(ev["pa"], 1)
                act.wait_ge(used, done("ac", 8, layer, it))
                A(gate_a[:, :, bass.ts(it, 256)], W1[:, :].rearrange("p (t c) -> p t c", t=TOK), ACT.Tanh,
                  scale=0.5).then_inc(free["W1"], 1)
                w(9)
                act.wait_ge(ev["lc"], ev_n("lc", layer, it + 1))
                for e in range(2):
                    for t in range(TOK):
                        s = lc[:, e, :, 0:P] if t == 0 else lc[:, e, :, P:3 * P]
                        k = 2 * t + e
                        A(s, s, ACT.Exp, bias=stat[:, 40 + k:41 + k], accum_out=stat[:, 44 + k:45 + k])
                act.drain().then_inc(ev["ec"], 1)
                w(10)
                act.wait_ge(used, done("ac", 10, layer, it))
                A(gate_c[:, :, bass.ts(it, 256)], W0[:, :].rearrange("p (t c) -> p t c", t=TOK), ACT.Tanh,
                  scale=0.5).then_inc(free["W0"], 1)
                act.drain().then_inc(ev["gates"], 2)
                act.wait_ge(used, done("ac", 14, layer, it - 1))

                def evacuate_pc(k):
                    b, n = PC_BANKS[k], 4 if k < 4 else 2
                    act.wait_ge(full[b], fill_n(b, f"pc{k}", layer, it))
                    A(pc[:, 4 * k:4 * k + n, :], bank[b][:, 0:n * P].rearrange("p (a t) -> p a t", a=n), ACT.Copy
                      ).then_inc(free[b], 1)
                    act.drain().then_inc(ev["pc"], 1)

                evacuate_pc(0)
                for t, b in enumerate(("S0", "S1")):
                    act.wait_ge(full[b], fill_n(b, f"oa{t}", layer, it))
                    i = A(y_hi[:, :, t * P:(t + 1) * P], bank[b][:, :].rearrange("p (h q) -> p h q", h=4),
                          ACT.Copy, scale=prm[:, G_CKV:G_CKV + 1])
                i.then_inc(ev["y_hi"], 1)
                for k in range(1, 5):
                    evacuate_pc(k)
                w(11, 12, 13)
                act.wait_ge(full["S0"], fill_n("S0", "ocT", layer, it))
                A(yc_hi[:, bass.ts(it, 1), :], S0[:, 0:SEQ].unsqueeze(1), ACT.Copy).then_inc(ev["oc"], 1)
                w(14)

            with act.Fori(0, DEPTH) as layer:
                w_split("f1pre", 0 - AHEAD, layer)
                w_split("f1pre", 1 - AHEAD, layer)
                norm(0, layer)
                w_split("f1pre", 2 - AHEAD, layer)
                w_split("f1pre", 3 - AHEAD, layer)
                norm_hi(0, layer)
                ffn("f1", layer)
                norm(1, layer)
                norm_hi(1, layer)
                mixer_start(layer)
                with act.Fori(1, GROUPS) as g:
                    scan(layer, g, False)
                scan(layer, GROUPS, True)
                with act.Fori(0, AC_STEPS) as it:
                    attention(layer, it)
                for k in range(4):
                    w_split("out", k, layer)
                for b, nm in enumerate(("W0", "W1", "S0", "S1")):
                    act.wait_ge(full[nm], fill_n(nm, "mT", layer))
                    A(h_hi[:, 2 * b:2 * b + 2, :], bank[nm][:, :].rearrange("p (k t) -> p k t", k=2),
                      ACT.Copy, scale=0.5).then_inc(ev["h_hi"], 1)
                for k in range(4, 12):
                    w_split("out", k, layer)
                norm(2, layer)
                norm_hi(2, layer)
                ffn("f2", layer)
                norm(3, layer)
                act.wait_ge(ple_loaded, layer * 16 + 16)
                A(c_hi[:, :, :], pin.rearrange("p (k t) -> p k t", k=2), ACT.Copy).then_inc(ev["cq_hi"], 1)
                norm_hi(3, layer)
                for k in range(6):
                    w_split("ple", k, layer)
                    if k in (3, 5):
                        b = ("W0", "W1")[k // 2 - 1]
                        n = k // 2 - 1
                        act.wait_ge(used, done("ple", 2 * n + 3, layer))
                        A(pg[:, :, n * 256:n * 256 + 256], bank[b][:, :].rearrange("p (t c) -> p t c", t=TOK),
                          ACT.Tanh, scale=0.5).then_inc(ev["gates"], 1)
                for n, b in ((2, "S0"), (3, "S1")):
                    act.wait_ge(used, done("ple", 2 * n + 3, layer))
                    A(pg[:, :, n * 256:n * 256 + 256], bank[b][:, :].rearrange("p (t c) -> p t c", t=TOK),
                      ACT.Tanh, scale=0.5).then_inc(ev["gates"], 1)
            norm(0, DEPTH)

        @block.vector
        def _(dve):
            TT, TS, STT = dve.tensor_tensor, dve.tensor_scalar, dve.scalar_tensor_tensor

            def w_split(seg, pos, layer, it=0):
                t, s, _, _ = look(seg, pos + AHEAD, it, layer)
                dve.wait_ge(hi_done, t + 1)
                TT(w_lo[s][:, :], raw[s][:, :], w_hi[s][:, :].bitcast(f32), SUB).then_inc(lo_done, 1)

            def norm(r, layer):
                if r == 0:
                    w_split("f1pre", 0 - AHEAD, layer)
                    w_split("f1pre", 1 - AHEAD, layer)
                    dve.drain()
                dve.wait_ge(ev["rstd"], ev_n("rstd", layer, r + 1))
                for t in range(TOK):
                    TS(diag[:, t, :], ident[:, :], stat[:, t:t + 1], None, MUL)
                dve.drain().then_inc(ev["diag"], 1)
                if r == 0:
                    w_split("f1pre", 2 - AHEAD, layer)
                    dve.wait_ge(prm_loaded, layer * 16 + 16)
                dve.wait_ge(ev["rstd_row"], ev_n("rstd_row", layer, r + 1))
                dve.tensor_copy(rstd_row, acc[0][0][:, 0:SEQ])
                dve.drain()

                def scaled(b):
                    for k in (2 * b, 2 * b + 1):
                        g = G_NORM + 8 * r + k
                        i = STT(normed[:, k, :], bank[("W0", "W1", "S0", "S1")[b]][:, (k % 2) * SEQ:(k % 2 + 1) * SEQ],
                                prm[:, g:g + 1], rstd_row, MUL, MUL)
                    i.then_inc(ev["normed"], 1)

                def lo(b):
                    dve.wait_ge(ev["h_hi"], ev_n("h_hi", layer, H_AT[r] + b + 1))
                    TT(h_lo[:, 2 * b:2 * b + 2, :], normed[:, 2 * b:2 * b + 2, :],
                       h_hi[:, 2 * b:2 * b + 2, :].bitcast(f32), SUB).then_inc(ev["h_lo"], 1)

                scaled(0)
                scaled(1)
                lo(0)
                scaled(2)
                lo(1)
                scaled(3)
                lo(2)
                lo(3)
                if r == 0:
                    w_split("f1pre", 3 - AHEAD, layer)

            def y_split(f, layer, j, c0):
                dve.wait_ge(ev["y_hi"], ev_n("y_hi", layer, j + (Y_AT[f] + 1)))
                TT(y_lo[:, c0:c0 + 2, :], act_f, y_hi[:, c0:c0 + 2, :].bitcast(f32), SUB).then_inc(ev["y_lo"], 1)

            def residual(seg, pos, layer, scale):
                dve.wait_ge(used, done(seg, pos, layer))
                for t in range(TOK):
                    for h in range(2):
                        i = STT(x[:, t, 512 * h:512 * h + 512], acc[t][h][:, :], scale,
                                x[:, t, 512 * h:512 * h + 512], MUL, ADD)
                    i.then_inc(ev["x_done"], 1)
                dve.drain().then_inc(ev["acc_free"], 1)

            def ffn(f, layer):
                def chunk(j, c, seg, pos, it=0):
                    b = ("W0", "W1")[c]
                    first = 0 if f == "f1" else 2 * PAIRS
                    dve.wait_ge(ev["ffn_tanh"], ev_n("ffn_tanh", layer, j * 2 + (first + c + 1)))
                    STT(ffn_t[:, c, :], ffn_t[:, c, :], 1.0, bank[b][:, 0:SEQ], ADD, MUL)
                    dve.drain()
                    dve.wait_ge(used, done(seg, pos, layer, it))
                    STT(act_f[:, c, :], ffn_t[:, c, :], 0.5, bank[b][:, SEQ:512], MUL, MUL
                        ).then_inc(free[b], 1)

                w_split(f + "pre", 0, layer)
                w_split(f + "pre", 1, layer)
                chunk(0, 0, f + "pre", 1)
                w_split(f + "pre", 2, layer)
                w_split(f + "pre", 3, layer)
                chunk(0, 1, f + "pre", 3)
                dve.drain().then_inc(ev["y_src"], 1)
                y_split(f, layer, 0, 0)
                with dve.Fori(0, PAIRS // 2) as i:
                    for u in range(2):
                        j, at = i * 2 + (1 + u), 6 * u
                        w_split(f + "loop", at, layer, i)
                        w_split(f + "loop", at + 1, layer, i)
                        dve.drain()
                        chunk(j, 0, f + "loop", at + 1, i)
                        w_split(f + "loop", at + 2, layer, i)
                        chunk(j, 1, f + "loop", at + 3, i)
                        dve.drain().then_inc(ev["y_src"], 1)
                        y_split(f, layer, j, 2 - 2 * u)
                        for k in (3, 4, 5):
                            w_split(f + "loop", at + k, layer, i)
                for k in range(2):
                    w_split(f + "tail", k, layer)
                residual(f + "tail", 1, layer, 0.5)

            def conv(layer, g, first):
                if first == 0:
                    dve.wait_ge(ev["taps"], ev_n("taps", layer, g + 1))
                    dve.wait_ge(ev["pre_x"], ev_n("pre_x", layer, g + 1))
                else:
                    dve.wait_ge(ev["pre_bc"], ev_n("pre_bc", layer, g + 1))
                for k in range(3):
                    if k:
                        dve.drain()
                    for c in range(first, first + 2):
                        STT(xbc[:, c, :], pre[:, c, k:k + SEQ], taps[:, 4 * c + k:4 * c + k + 1], xbc[:, c, :],
                            MUL, ADD)
                dve.drain().then_inc(ev["conv"], 1)

            def conv_silu(layer, g, c0):
                dve.wait_ge(ev["conv_tanh"], ev_n("conv_tanh", layer, 2 * g + (c0 // 2 + 1)))
                i = STT(xbc[:, c0:c0 + 2, :], conv_t[:, c0:c0 + 2, :], 1.0, xbc[:, c0:c0 + 2, :], ADD, MUL)
                if c0 == 2:
                    dve.drain().then_inc(ev["xbc"], 1)

            def gate_z(layer, g):
                dve.wait_ge(ev["z_tanh"], ev_n("z_tanh", layer, g + 1))
                STT(zz, zz, 1.0, W0[:, :].rearrange("p (t c) -> p t c", t=TOK), ADD, MUL
                    ).then_inc(free["W0"], 1)
                dve.drain().then_inc(ev["zz"], 1)

            def mixer_start(layer):
                split = iter(range(27))

                def w(n):
                    for _ in range(n):
                        w_split("m0", next(split), layer)
                grp = prm[:, G_GRP:G_GRP + GROUPS * GRP].rearrange("p (g n) -> p g n", g=GROUPS)[:, :, 0:20]
                TS(grp, grp, 0.5, None, MUL)
                w(4)
                dve.drain()
                dve.wait_ge(ev["small"], ev_n("small", layer, 2))
                TT(dt_a[:, 0, :].rearrange("p (t h) -> p t h", t=TOK), small[:, :, 456:488],
                   prm[:, G_DTB:G_DTB + 32].unsqueeze(1).broadcast_to([P, TOK, 32]), ADD)
                dve.tensor_copy(ki2.rearrange("p t (e c) -> p t e c", e=2),
                                small[:, :, 384:448].unsqueeze(2).broadcast_to([P, TOK, 2, IDX_DIM]))
                TS(wix[:, :, :], small[:, :, 448:456], float((IDX_HEADS * IDX_DIM) ** -0.5), None, MUL)
                dve.drain()
                STT(dt_a[:, 1, :], dt_a[:, 0, :], -1.0, dt_a[:, 0, :], MUL, MAX)
                dve.drain().then_inc(ev["dt_in"], 1)
                w(2)
                dve.wait_ge(ev["prep_rstd"], ev_n("prep_rstd", layer, 1))
                for t in range(TOK):
                    TS(cqn[:, t, :], small[:, t, 0:256], stat[:, 4 + t:5 + t], None, MUL)
                    TS(kvn[:, t, :], small[:, t, 256:384], stat[:, 6 + t:7 + t], None, MUL)
                dve.drain().then_inc(ev["prep_n"], 1)
                w(2)
                dve.wait_ge(ev["dt_ln"], ev_n("dt_ln", layer, 1))
                STT(dts[:, :, :].rearrange("p t h -> p (t h)"), dt_a[:, 0, :], 0.0, dt_a[:, 1, :], MAX, ADD)
                dve.drain()
                STT(da[:, :, :], dts[:, :, :], -1.0,
                    prm[:, G_EXPA:G_EXPA + 32].unsqueeze(1).broadcast_to([P, TOK, 32]), MUL, MUL)
                dve.drain().then_inc(ev["da"], 1)
                w(8)
                dve.wait_ge(full["S0"], fill_n("S0", "cqT", layer))
                TT(cqf.rearrange("p (k t) -> p k t", k=2), S0[:, :].rearrange("p (k t) -> p k t", k=2),
                   prm[:, G_CQ:G_CQ + 2].unsqueeze(2).broadcast_to([P, 2, SEQ]), MUL).then_inc(free["S0"], 1)
                dve.drain().then_inc(ev["cq_gained"], 1)
                dve.wait_ge(full["S1"], fill_n("S1", "kvT", layer))
                TS(kv_t[:, :], S1[:, 0:SEQ], prm[:, G_CKV:G_CKV + 1], None, MUL)
                dve.tensor_copy(ki_t[:, :], S1[:, SEQ:512]).then_inc(free["S1"], 1)
                dve.drain().then_inc(ev["kv"], 1)
                dve.wait_ge(ev["cq_hi"], ev_n("cq_hi", layer, 1))
                TT(c_lo[:, :, :], cqf.rearrange("p (k t) -> p k t", k=2), c_hi[:, :, :].bitcast(f32), SUB
                   ).then_inc(ev["cq_lo"], 1)
                w(4)
                conv(layer, 0, 0)
                conv(layer, 0, 2)
                w(1)
                conv_silu(layer, 0, 0)
                conv_silu(layer, 0, 2)
                w(2)
                gate_z(layer, 0)
                for k in range(6):
                    dve.wait_ge(ev["relu"], ev_n("relu", layer, k + 1))
                    heads, width, at, t = indexer_fill(k)
                    for e, h in enumerate(heads):
                        acc_in = causal if h == 0 else score
                        STT(score[:, at:at + width], relu[:, k % 2, e * width:(e + 1) * width],
                            wix[:, t, h:h + 1], acc_in[:, at:at + width], MUL, ADD)
                        dve.drain()
                    dve.drain().then_inc(ev["weighted"], 1)
                    if k == 1:
                        w(2)

            def top_round(layer):
                for t, (a, n) in enumerate(((0, P), (P, SEQ))):
                    dve.max(top8[:, t, :], score[:, a:a + n])
                dve.drain()
                for t, (a, n) in enumerate(((0, P), (P, SEQ))):
                    dve.match_replace(out=score[:, a:a + n], in_to_replace=top8[:, t, :],
                                      in_values=score[:, a:a + n], imm_value=SCORE_TAKEN)
                dve.drain()

            def scan(layer, g, last):
                sfx = "_last" if last else ""
                q = 0 if last else g - 1
                gi = g - 1
                S0g = S0[:, :].rearrange("p (t h c) -> p t h c", t=TOK, h=HG)
                hd = [P, TOK, HG, HEADDIM]
                heads = bass.ts(gi, HG)
                if last:
                    dve.wait_ge(ev["ecum"], ev_n("ecum", layer, 1))
                dve.wait_ge(full["S0"], fill_n("S0", f"xT{sfx}", layer, q))
                xdt4 = xdt.rearrange("p t (h c) -> p t h c", h=HG)
                xd4 = xd.rearrange("p t (h c) -> p t h c", h=HG)
                skip = prm[:, bass.ds(gi * GRP + (G_GRP + 22), 4)]
                TT(xdt4, S0g, dts[:, :, heads].unsqueeze(3).broadcast_to(hd), MUL)
                TT(xd4, S0g, skip.unsqueeze(1).unsqueeze(3).broadcast_to(hd), MUL).then_inc(free["S0"], 1)
                dve.wait_ge(full["S1"], fill_n("S1", f"bcb{sfx}", layer, q))
                dve.tensor_copy(b_tok, S1[:, 0:P])
                TT(cbm, S1[:, P:3 * P].rearrange("p (t i) -> p t i", t=TOK),
                   upto[:, :].unsqueeze(1).broadcast_to([P, TOK, P]), MUL).then_inc(free["S1"], 1)
                dve.drain()
                TT(xw.rearrange("p (h c) -> p h c", h=HG), xdt4[:, 0, :, :],
                   wl[:, heads].unsqueeze(2).broadcast_to([P, HG, HEADDIM]), MUL)
                dve.drain().then_inc(ev["ssd_in"], 1)
                for t in range(TOK):
                    dve.wait_ge(ev["decay"], ev_n("decay", layer, gi * 2 + t + 1))
                    d4 = decay[:, t, :].rearrange("p (h i) -> p h i", h=HG)
                    TT(d4, d4, cbm[:, t, :].unsqueeze(1).broadcast_to([P, HG, P]), MUL)
                dve.drain().then_inc(ev["scan_w"], 1)
                for k in (-2, -1):
                    w_split("btail" if last else "bloop", k, layer, q)
                dve.wait_ge(full["S0"], fill_n("S0", f"ydiag{sfx}", layer, q))
                TT(ysum, S0[:, :].rearrange("p (t c) -> p t c", t=TOK), xd, ADD).then_inc(free["S0"], 1)
                dve.wait_ge(full["S1"], fill_n("S1", f"yoff{sfx}", layer, q))
                TT(yoffs.rearrange("p (h c) -> p h c", h=HG), S1[:, 0:256].rearrange("p (h c) -> p h c", h=HG),
                   ecum[:, heads].unsqueeze(2).broadcast_to([P, HG, HEADDIM]), MUL).then_inc(free["S1"], 1)
                dve.drain()
                TT(ysum[:, 1, :], ysum[:, 1, :], yoffs, ADD)
                dve.drain()
                STT(ysum, zz, 0.5, ysum, MUL, MUL)
                dve.drain().then_inc(ev["y_sum"], 1)
                for k in (0, 1):
                    w_split("btail" if last else "bloop", k, layer, q)
                top_round(layer)
                if not last:
                    conv(layer, g, 0)
                w_split("btail" if last else "bloop", 2, layer, q)
                dve.wait_ge(ev["y_hi"], ev_n("y_hi", layer, gi + (Y_AT["b"] + 1)))
                for k in range(2):
                    i = STT(y_lo[:, k, :], S1[:, k * SEQ:(k + 1) * SEQ],
                            prm[:, bass.ds(gi * GRP + (G_GRP + 20 + k), 1)], y_hi[:, k, :].bitcast(f32), MUL, SUB)
                i.then_inc(ev["y_lo"], 1)
                w_split("btail" if last else "bloop", 3, layer, q)
                if not last:
                    conv(layer, g, 2)
                    conv_silu(layer, g, 0)
                    conv_silu(layer, g, 2)
                    gate_z(layer, g)
                w_split("btail" if last else "bloop", 4, layer, q)
                w_split("btail" if last else "bloop", 5, layer, q)

            def gated(layer, gate, gates_at):
                dve.wait_ge(ev["gates"], ev_n("gates", layer, gates_at))
                for t in range(TOK):
                    for h in range(2):
                        c = slice(512 * h, 512 * h + 512)
                        STT(gate[:, t, c], gate[:, t, c], 1.0, acc[t][h][:, :], ADD, MUL)
                dve.drain().then_inc(ev["acc_free"], 1)

            def attention(layer, it):
                def w(*ps):
                    for p in ps:
                        w_split("ac", p, layer, it)
                w(0, 1, 2)
                dve.drain()
                dve.wait_ge(bias_loaded, layer * (64 * AC_STEPS) + (it * 64 + 64))
                dve.wait_ge(ev["pc"], ev_n("pc", layer, it * 5))
                scale = float(A_DC ** -0.5)
                for k, (b, hs) in enumerate((("S0", 0), ("S1", 2))):
                    dve.wait_ge(full[b], fill_n(b, f"la{k}", layer, it))
                    STT(la[:, hs:hs + 2, P:3 * P], bank[b][:, :].rearrange("p (h s) -> p h s", h=2), scale,
                        bias[:, hs:hs + 2, :], MUL, ADD).then_inc(free[b], 1)
                w(3, 4)
                dve.wait_ge(full["S0"], fill_n("S0", "la2", layer, it))
                STT(la[:, :, 0:P], S0[:, :].rearrange("p (h s) -> p h s", h=4), scale,
                    bias[:, 0:4, P:SEQ], MUL, ADD).then_inc(free["S0"], 1)
                dve.drain()
                TT(la, la, score[:, :].unsqueeze(1).broadcast_to([P, 4, 3 * P]), ADD)
                dve.drain()
                for t in range(TOK):
                    s = la[:, :, 0:P] if t == 0 else la[:, :, P:3 * P]
                    dve.tensor_reduce(stat[:, 16 + 4 * t:20 + 4 * t], s, AX.X, MAX)
                dve.drain()
                TS(stat[:, 16:24], stat[:, 16:24], -1.0, None, MUL)
                dve.drain().then_inc(ev["la"], 1)
                scale = float(C_DIM ** -0.5)
                for g in range(CG):
                    for e, b in enumerate(("S0", "S1")):
                        dve.wait_ge(full[b], fill_n(b, f"lc{2 * g + e}", layer, it))
                        STT(lc[:, e, g, 0:P], bank[b][:, 0:P], scale, bias[:, 4 + 2 * g + e, P:SEQ], MUL, ADD)
                        STT(lc[:, e, g, P:3 * P], bank[b][:, P:3 * P], scale, bias[:, 4 + 2 * g + e, :],
                            MUL, ADD).then_inc(free[b], 1)
                w(5)
                dve.wait_ge(ev["ea"], ev_n("ea", layer, it + 1))
                dve.reciprocal(stat[:, 32:40], stat[:, 24:32])
                dve.drain()
                for t in range(TOK):
                    s, n = (la[:, :, 0:P], P) if t == 0 else (la[:, :, P:3 * P], SEQ)
                    TT(s, s, stat[:, 32 + 4 * t:36 + 4 * t].unsqueeze(2).broadcast_to([P, 4, n]), MUL)
                dve.drain().then_inc(ev["na"], 1)
                w(6, 7)
                for e in range(2):
                    for t in range(TOK):
                        s = lc[:, e, :, 0:P] if t == 0 else lc[:, e, :, P:3 * P]
                        dve.tensor_reduce(stat[:, 40 + 2 * t + e:41 + 2 * t + e], s, AX.XY, MAX)
                dve.drain()
                TS(stat[:, 40:44], stat[:, 40:44], -1.0, None, MUL)
                dve.drain().then_inc(ev["lc"], 1)
                w(8, 9)
                w(10)
                dve.wait_ge(ev["y_hi"], ev_n("y_hi", layer, it + (Y_AT["a"] + 1)))
                for t, b in enumerate(("S0", "S1")):
                    STT(y_lo[:, :, t * P:(t + 1) * P], bank[b][:, :].rearrange("p (h q) -> p h q", h=4),
                        prm[:, G_CKV:G_CKV + 1], y_hi[:, :, t * P:(t + 1) * P].bitcast(f32), MUL, SUB
                        ).then_inc(free[b], 1)
                dve.drain().then_inc(ev["y_lo"], 1)
                dve.wait_ge(ev["ec"], ev_n("ec", layer, it + 1))
                dve.reciprocal(stat[:, 48:52], stat[:, 44:48])
                w(11, 12)
                dve.drain()
                dve.wait_ge(full["S1"], fill_n("S1", "oc", layer, it))
                TT(oc_f.rearrange("p t (e c) -> p t e c", e=2),
                   S1[:, 0:2 * P].rearrange("p (t e c) -> p t e c", t=TOK, e=2),
                   stat[:, 48:52].rearrange("p (t e) -> p t e", t=TOK).unsqueeze(3)
                   .broadcast_to([P, TOK, 2, C_DIM]), MUL).then_inc(free["S1"], 1)
                dve.drain().then_inc(ev["nc_"], 1)
                w(13)
                dve.wait_ge(ev["oc"], ev_n("oc", layer, it + 1))
                TT(yc_lo[:, bass.ts(it, 1), :], S0[:, 0:SEQ].unsqueeze(1),
                   yc_hi[:, bass.ts(it, 1), :].bitcast(f32), SUB).then_inc(free["S0"], 1)
                dve.drain().then_inc(ev["oc_lo"], 1)
                w(14)

            dve.sem_inc(lo_done, SLOTS)
            for name in SEEDED:
                dve.sem_inc(ev[name], 1)
            for b in bank:
                dve.sem_inc(free[b], 1)
            dve.memset(zeros[:, :], 0.0).then_inc(cleared, 1)
            dve.memset(ones[:, :], 1.0).then_inc(cleared, 1)
            dve.memset(pre[:, :, 0:3], 0.0)
            for v in range(4):
                n = A_HEADS if v == 0 else C_HEADS
                dve.wait_ge(tables, v + 1)
                dve.tensor_copy(rb[0:n, v, :], acc[v // 2][v % 2][0:n, 0:ROW]).then_inc(tables_sb, 1)

            with dve.Fori(0, DEPTH) as layer:
                norm(0, layer)
                ffn("f1", layer)
                norm(1, layer)
                dve.drain()
                dve.memset(pre[:, :, 0:3], 0.0)
                mixer_start(layer)
                with dve.Fori(1, GROUPS) as g:
                    scan(layer, g, False)
                scan(layer, GROUPS, True)
                TS(score[:, :], score[:, :], SCORE_CUT, MASKED, ALU.is_ge, MUL)
                dve.wait_ge(used, done("btail", 5, layer))
                gated(layer, gate_b, 8)
                with dve.Fori(0, AC_STEPS) as it:
                    attention(layer, it)
                dve.wait_ge(ev["branch_a"], ev_n("branch_a", layer, 1))
                gated(layer, gate_a, 8 + 2 * AC_STEPS)
                TT(gate_b[:, :, :], gate_b[:, :, :], gate_a[:, :, :], ADD)
                for k in range(4):
                    w_split("out", k, layer)
                dve.wait_ge(used, done("out", 3, layer))
                for h in range(2):
                    c = slice(512 * h, 512 * h + 512)
                    for t in range(TOK):
                        nm = ("W0", "W1", "S0", "S1")[2 * h + t]
                        STT(gate_c[:, t, c], gate_c[:, t, c], 1.0, bank[nm][:, :], ADD, MUL).then_inc(free[nm], 1)
                    dve.drain()
                    TT(gate_b[:, :, c], gate_b[:, :, c], gate_c[:, :, c], ADD)
                    dve.drain().then_inc(ev["merged"], 1)
                for b, nm in enumerate(("W0", "W1", "S0", "S1")):
                    dve.wait_ge(ev["h_hi"], ev_n("h_hi", layer, 8 + b + 1))
                    STT(h_lo[:, 2 * b:2 * b + 2, :], bank[nm][:, :].rearrange("p (k t) -> p k t", k=2), 0.5,
                        h_hi[:, 2 * b:2 * b + 2, :].bitcast(f32), MUL, SUB).then_inc(ev["h_lo"], 1)
                for k in range(4, 12):
                    w_split("out", k, layer)
                residual("out", 11, layer, 1.0)
                norm(2, layer)
                ffn("f2", layer)
                dve.wait_ge(ev["cq_hi"], ev_n("cq_hi", layer, 2))
                TT(c_lo[:, :, :], pin.rearrange("p (k t) -> p k t", k=2), c_hi[:, :, :].bitcast(f32), SUB
                   ).then_inc(ev["cq_lo"], 1)
                norm(3, layer)
                for k in range(6):
                    w_split("ple", k, layer)
                dve.wait_ge(used, done("ple", 1, layer))
                for n in range(4):
                    c, a = slice(256 * n, 256 * n + 256), slice(256 * (n % 2), 256 * (n % 2) + 256)
                    dve.wait_ge(ev["gates"], ev_n("gates", layer, 16 + n + 1))
                    for t in range(TOK):
                        STT(pg[:, t, c], pg[:, t, c], 1.0, acc[t][n // 2][:, a], ADD, MUL)
                    dve.drain()
                    for t in range(TOK):
                        i = STT(x[:, t, c], pg[:, t, c], 0.5, x[:, t, c], MUL, ADD)
                        if n == 3:
                            i.then_inc(ev["x_done"], 1)
                dve.drain().then_inc(ev["acc_free"], 1)
            dve.wait_ge(ev["rstd"], 4 * DEPTH + 1)
            dve.wait_ge(fgain_loaded, 16)
            for t in range(TOK):
                STT(x[:, t, :], x[:, t, :], stat[:, t:t + 1], fgain, MUL, MUL).then_inc(final, 1)

        @block.tensor
        def _(pe):
            mm = pe.matmul

            def three(o, lh, ll, rh, rl, start, stop):
                mm(o, lh, rh, start=start, stop=False)
                mm(o, lh, rl, start=False, stop=False)
                return mm(o, ll, rh, start=False, stop=stop)

            def weight(seg, pos, layer, it=0):
                t, s, _, _ = tile_numbers(seg, pos, it, layer)
                pe.wait_ge(lo_done, t + 1 + SLOTS)
                return s

            def fill(b, name, layer, it=0):
                pe.wait_ge(free[b], free_n(b, name, layer, it))
                return bank[b]

            def features(o, seg, pos, layer, it=0, norm_r=None):
                s = weight(seg, pos, layer, it)
                for k in range(KD):
                    h_part(norm_r, k, layer)
                    c = slice(k * P, (k + 1) * P)
                    last = three(o, w_hi[s][:, c], w_lo[s][:, c], h_hi[:, k, :], h_lo[:, k, :],
                                 k == 0, k == KD - 1)
                last.then_inc(used, 1)
                return last

            def tokens(b, seg, pos, layer, it=0, norm_r=None):
                s = [weight(seg, pos + i, layer, it) for i in range(2)]
                for t in range(TOK):
                    for k in range(KD):
                        h_part(norm_r if t == 0 else None, k, layer)
                        sl, c = s[k // 4], slice((k % 4) * 256, (k % 4) * 256 + 256)
                        o = b[:, t * 256:t * 256 + 256]
                        hh, hl = (a[:, k, t * P:(t + 1) * P] for a in (h_hi, h_lo))
                        mm(o, hh, w_hi[sl][:, c], start=k == 0, stop=False)
                        mm(o, hh, w_lo[sl][:, c], start=False, stop=False)
                        last = mm(o, hl, w_hi[sl][:, c], start=False, stop=k == KD - 1)
                        if t == TOK - 1 and k % 4 == 3:
                            last.then_inc(used, 1)

            def rows(yh, yl, seg, pos, layer, it=0, start=False, stop=False, into=acc):
                s = weight(seg, pos, layer, it)
                for t in range(TOK):
                    a, b = yh[:, t * P:(t + 1) * P], yl[:, t * P:(t + 1) * P]
                    for h in range(2):
                        c = slice(512 * h, 512 * h + 512)
                        mm(into[t][h][:, :], a, w_hi[s][:, c], start=start, stop=False)
                        mm(into[t][h][:, :], a, w_lo[s][:, c], start=False, stop=False)
                        last = mm(into[t][h][:, :], b, w_hi[s][:, c], start=False, stop=stop)
                last.then_inc(used, 1)

            def acc_zero(use, layer):
                pe.wait_ge(ev["acc_free"], ev_n("acc_free", layer, ACC_USES[use]))
                for t in range(TOK):
                    for h in range(2):
                        mm(acc[t][h][:, :], zeros[:, 0:P], zeros[:, :], start=True, stop=False)

            def turn_rows(src, name, layer):
                for b, nm in enumerate(("W0", "W1", "S0", "S1")):
                    pe.wait_ge(ev["merged"], ev_n("merged", layer, b // 2 + 1))
                    o = fill(nm, name, layer)
                    for k in range(2):
                        for t in range(TOK):
                            c = (2 * b + k) * P
                            last = pe.transpose(o[:, k * SEQ + t * P:k * SEQ + (t + 1) * P],
                                                src[:, t, c:c + P], ident[:, :])
                    last.then_inc(full[nm], 1)

            def norm(r, layer):
                banks = [fill(nm, f"norm{r}", layer) for nm in ("W0", "W1", "S0", "S1")]
                for t in range(TOK):
                    pe.wait_ge(ev["x_done"], ev_n("x_done", layer, 2 * (r - 1) + t + 1 if r else 0))
                    for c in range(KD):
                        at = (c % 2) * SEQ + t * P
                        pe.transpose(banks[c // 2][:, at:at + P], x[:, t, c * P:(c + 1) * P], ident[:, :])
                pe.wait_ge(ev["diag"], ev_n("diag", layer, r + 1))
                pe.wait_ge(ev["acc_free"], ev_n("acc_free", layer, ACC_USES[("f1", "b", "f2", "ple")[r]]))
                mm(acc[0][0][:, 0:SEQ], ones[:, :], diag[:, :, :].rearrange("p t q -> p (t q)"), start=True, stop=True
                   ).then_inc(ev["rstd_row"], 1)

            def h_part(r, k, layer):
                if r is not None and k % 2 == 0:
                    pe.wait_ge(ev["h_lo"], ev_n("h_lo", layer, H_AT[r] + k // 2 + 1))

            def ffn(f, layer):
                def chunk(seg, pos, j, c, it=0, norm_r=None):
                    b, name = (("W0", f + "even"), ("W1", f + "odd"))[c]
                    o = fill(b, name, layer, j)
                    features(o[:, 0:SEQ], seg, pos, layer, it, norm_r)
                    features(o[:, SEQ:512], seg, pos + 1, layer, it)

                def down(seg, pos, j, c0, it=0, stop=False):
                    pe.wait_ge(ev["y_lo"], ev_n("y_lo", layer, j + (Y_AT[f] + 1)))
                    for k in range(2):
                        rows(y_hi[:, c0 + k, :], y_lo[:, c0 + k, :], seg, pos + k, layer, it, stop=stop and k == 1)

                pe.wait_ge(ev["h_lo"], ev_n("h_lo", layer, H_AT[0 if f == "f1" else 2] + 1))
                chunk(f + "pre", 0, 0, 0, norm_r=0 if f == "f1" else 2)
                acc_zero(f, layer)
                chunk(f + "pre", 2, 0, 1)
                with pe.Fori(0, PAIRS // 2) as i:
                    for u in range(2):
                        j, at = i * 2 + (1 + u), 6 * u
                        chunk(f + "loop", at, j, 0, i)
                        chunk(f + "loop", at + 2, j, 1, i)
                        down(f + "loop", at + 4, j - 1, 2 * u, i)
                down(f + "tail", 0, PAIRS - 1, 0, stop=True)

            def project_x(name, seg, pos, layer, it=0):
                o = fill("W0", name, layer, it)
                features(o[:, 0:SEQ], seg, pos, layer, it)
                features(o[:, SEQ:512], seg, pos + 1, layer, it)

            def project_bc(name, seg, pos, layer, it=0):
                o = fill("W1", name, layer, it)
                features(o[:, 0:SEQ], seg, pos, layer, it)
                features(o[:, SEQ:512], seg, pos + 1, layer, it)

            def project_tok(b, name, seg, pos, layer, it=0):
                o = fill(b, name, layer, it)
                tokens(o, seg, pos, layer, it)

            def mixer_start(layer):
                pe.wait_ge(ev["h_lo"], ev_n("h_lo", layer, H_AT[1] + 1))
                o = fill("W0", "small0", layer)
                tokens(o, "m0", 0, layer, norm_r=1)
                project_tok("W1", "small1", "m0", 2, layer)
                for u in range(6):
                    b, name = (("W0", "v_even"), ("W1", "v_odd"))[u % 2]
                    tokens_at(b, name, "m0", 4 + 2 * u, layer, u // 2)
                pe.wait_ge(ev["prep_n"], ev_n("prep_n", layer, 1))
                o = fill("S0", "cqT", layer)
                for k in range(2):
                    for t in range(TOK):
                        last = pe.transpose(o[:, k * SEQ + t * P:k * SEQ + (t + 1) * P],
                                            cqn[:, t, k * P:(k + 1) * P], ident[:, :])
                last.then_inc(full["S0"], 1)
                o = fill("S1", "kvT", layer)
                for t in range(TOK):
                    pe.transpose(o[:, t * P:(t + 1) * P], kvn[:, t, :], ident[:, :])
                for t in range(TOK):
                    last = pe.transpose(o[:, SEQ + t * P:SEQ + (t + 1) * P], ki2[:, t, :], ident[:, :])
                last.then_inc(full["S1"], 1)
                pe.wait_ge(ev["da"], ev_n("da", layer, 1))
                o = fill("S0", "cum", layer)
                mm(o[:, 0:32], upto[:, :], da[:, 1, :], start=True, stop=True)
                mm(o[:, 32:64], after[:, :], da[:, 0, :], start=True, stop=True).then_inc(full["S0"], 1)
                project_x("x_first", "m0", 16, layer)
                project_bc("bc_first", "m0", 18, layer)
                pe.wait_ge(ev["cq_lo"], ev_n("cq_lo", layer, 1))
                s = weight("m0", 20, layer)
                for c, b in enumerate(("S0", "S1")):
                    o = fill(b, f"qi{c}", layer)
                    for e in range(2):
                        for kk in range(2):
                            at = kk * 512 + (2 * c + e) * P
                            cs = slice(at, at + P)
                            last = three(o[:, e * SEQ:(e + 1) * SEQ], w_hi[s][:, cs], w_lo[s][:, cs],
                                         c_hi[:, kk, :], c_lo[:, kk, :], kk == 0, kk == 1)
                    last.then_inc(full[b] if c == 0 else used, 1)
                tokens_at("W0", "z_first", "m0", 21, layer)
                pe.wait_ge(ev["qi"], ev_n("qi", layer, 2))
                pe.wait_ge(ev["kv"], ev_n("kv", layer, 1))
                for k in range(6):
                    b, name = (("S0", "sc1_even"), ("S1", "sc1_odd"))[k % 2] if k < 4 else \
                        (("S0", "sc0_even"), ("S1", "sc0_odd"))[k % 2]
                    o = fill(b, name, layer, k // 2 if k < 4 else 0)
                    heads, width, _, t = indexer_fill(k)
                    r = slice((k % 2) * IDX_DIM, (k % 2 + 1) * IDX_DIM)
                    for e, h in enumerate(heads):
                        last = mm(o[:, e * width:(e + 1) * width], qi[r, h // 2, t * P:(t + 1) * P],
                                  ki_t[r, 0:width], start=True, stop=True)
                    last.then_inc(full[b], 1)
                    if k == 1:
                        tokens_at("W1", "gb0", "m0", 23, layer)
                    if k == 3:
                        tokens_at("W0", "gb1", "m0", 25, layer)

            def tokens_at(b, name, seg, pos, layer, it=0):
                o = fill(b, name, layer, it)
                tokens(o, seg, pos, layer)

            def scan(layer, g, last):
                sfx = "_last" if last else ""
                q = 0 if last else g - 1
                gi = g - 1
                pe.wait_ge(ev["xbc"], ev_n("xbc", layer, g))
                o = fill("S0", f"xT{sfx}", layer, q)
                for t in range(TOK):
                    for c in range(2):
                        i = pe.transpose(o[:, t * 256 + c * P:t * 256 + (c + 1) * P],
                                         xbc[:, c, t * P:(t + 1) * P], ident[:, :])
                i.then_inc(full["S0"], 1)
                o = fill("S1", f"bcb{sfx}", layer, q)
                pe.transpose(o[:, 0:P], xbc[:, 2, 0:P], ident[:, :])
                for t in range(TOK):
                    ts = slice(t * P, (t + 1) * P)
                    i = mm(o[:, P + t * P:2 * P + t * P], xbc[:, 2, ts], xbc[:, 3, ts], start=True, stop=True)
                i.then_inc(full["S1"], 1)
                pe.wait_ge(ev["dau"], ev_n("dau", layer, g))
                for t, b in enumerate(("W0", "W1")):
                    o = fill(b, f"seg{t}{sfx}", layer, q)
                    mm(o[:, :], after[:, :], dau[:, t, :], start=True, stop=True).then_inc(full[b], 1)
                if last:
                    tokens_at("W0", "gb2", "btail", 0, layer)
                else:
                    project_x("x", "bloop", 0, layer, q)
                pe.wait_ge(ev["ssd_in"], ev_n("ssd_in", layer, g))
                o = fill("S1", f"state{sfx}", layer, q)
                mm(o[:, 0:256], b_tok, xw, start=True, stop=True).then_inc(full["S1"], 1)
                pe.wait_ge(ev["scan_w"], ev_n("scan_w", layer, g))
                o = fill("S0", f"ydiag{sfx}", layer, q)
                for t in range(TOK):
                    for h in range(HG):
                        c = t * 256 + h * HEADDIM
                        i = mm(o[:, c:c + HEADDIM], decay[:, t, h * P:(h + 1) * P],
                               xdt[:, t, h * HEADDIM:(h + 1) * HEADDIM], start=True, stop=True)
                i.then_inc(full["S0"], 1)
                pe.wait_ge(ev["state"], ev_n("state", layer, g))
                o = fill("S1", f"yoff{sfx}", layer, q)
                mm(o[:, 0:256], xbc[:, 3, P:SEQ], st, start=True, stop=True).then_inc(full["S1"], 1)
                if last:
                    tokens_at("W1", "gb3", "btail", 2, layer)
                else:
                    project_bc("bc", "bloop", 2, layer, q)
                pe.wait_ge(ev["yn"], ev_n("yn", layer, g))
                o = fill("S1", f"yT{sfx}", layer, q)
                for k in range(2):
                    for t in range(TOK):
                        i = pe.transpose(o[:, k * SEQ + t * P:k * SEQ + (t + 1) * P],
                                         ysum[:, t, k * P:(k + 1) * P], ident[:, :])
                i.then_inc(full["S1"], 1)
                if not last:
                    project_tok("W0", "z", "bloop", 4, layer, q)
                pe.wait_ge(ev["y_lo"], ev_n("y_lo", layer, gi + (Y_AT["b"] + 1)))
                seg, pos = ("btail", 4) if last else ("bloop", 6)
                for k in range(2):
                    rows(y_hi[:, k, :], y_lo[:, k, :], seg, pos + k, layer, q, stop=last and k == 1)

            def attention(layer, it, first=False):
                s = weight("ac", 0, layer, it)
                for c, b in enumerate(("W0", "W1")):
                    o = fill(b, f"qa{c}", layer, it)
                    for e in range(2):
                        h = 2 * c + e
                        for kk in range(2):
                            cs = slice(kk * 512 + h * P, kk * 512 + (h + 1) * P)
                            i = three(o[:, e * SEQ:(e + 1) * SEQ], w_hi[s][:, cs], w_lo[s][:, cs],
                                      c_hi[:, kk, :], c_lo[:, kk, :], kk == 0, kk == 1)
                    i.then_inc(full[b] if c == 0 else used, 1)

                def project_qk(g):
                    b = ("W0", "W1", "W0")[g]
                    o = fill(b, f"qk{g}", layer, it)
                    features(o[:, 0:SEQ], "ac", 1 + 2 * g, layer, it)
                    features(o[:, SEQ:512], "ac", 2 + 2 * g, layer, it)

                project_qk(0)
                pe.wait_ge(ev["qa"], ev_n("qa", layer, it + 1))
                for k, (b, hs) in enumerate((("S0", 0), ("S1", 2))):
                    o = fill(b, f"la{k}", layer, it)
                    for e in range(2):
                        i = mm(o[:, e * SEQ:(e + 1) * SEQ], qa[:, hs + e, P:SEQ], kv_t[:, :],
                               start=True, stop=True)
                    i.then_inc(full[b], 1)
                project_qk(1)
                o = fill("S0", "la2", layer, it)
                for h in range(4):
                    i = mm(o[:, h * P:(h + 1) * P], qa[:, h, 0:P], kv_t[:, 0:P], start=True, stop=True)
                i.then_inc(full["S0"], 1)
                project_qk(2)
                for g in range(CG):
                    pe.wait_ge(ev["qk"], ev_n("qk", layer, it * 3 + (g + 1)))
                    for e, b in enumerate(("S0", "S1")):
                        r = slice(e * C_DIM, (e + 1) * C_DIM)
                        o = fill(b, f"lc{2 * g + e}", layer, it)
                        mm(o[:, 0:P], qk[r, g, 0, 0:P], qk[r, g, 1, 0:P], start=True, stop=True)
                        mm(o[:, P:3 * P], qk[r, g, 0, P:SEQ], qk[r, g, 1, :], start=True, stop=True
                           ).then_inc(full[b], 1)
                project_tok("W1", "ga", "ac", 7, layer, it)
                pe.wait_ge(ev["na"], ev_n("na", layer, it + 1))
                for k in range(3):
                    b = ("W0", "S0", "S1")[k]
                    o = fill(b, f"pa{k}", layer, it)
                    for h in range(4):
                        i = pe.transpose(o[:, h * P:(h + 1) * P], la[:, h, k * P:(k + 1) * P], ident[:, :])
                    i.then_inc(full[b], 1)
                project_tok("W0", "gc", "ac", 9, layer, it)
                pe.wait_ge(ev["ec"], ev_n("ec", layer, it + 1))
                blocks = [(k, e, g) for k in range(3) for e in range(2) for g in range(CG)]

                def turn_pc(n):
                    b = PC_BANKS[n]
                    o = fill(b, f"pc{n}", layer, it)
                    for i_, (k, e, g) in enumerate(blocks[4 * n:4 * n + 4]):
                        i = pe.transpose(o[:, i_ * P:(i_ + 1) * P], lc[:, e, g, k * P:(k + 1) * P], ident[:, :])
                    i.then_inc(full[b], 1)

                turn_pc(0)
                pe.wait_ge(ev["pa"], ev_n("pa", layer, it * 3 + 3))
                o = fill("S0", "oa0", layer, it)
                mm(o[:, :], kvn[:, 0, :], pa[:, 0, :], start=True, stop=True).then_inc(full["S0"], 1)
                o = fill("S1", "oa1", layer, it)
                mm(o[:, :], kvn[:, 0, :], pa[:, 1, :], start=True, stop=False)
                mm(o[:, :], kvn[:, 1, :], pa[:, 2, :], start=False, stop=True).then_inc(full["S1"], 1)
                for n in range(1, 5):
                    turn_pc(n)
                pe.wait_ge(ev["y_lo"], ev_n("y_lo", layer, it + (Y_AT["a"] + 1)))
                if first:
                    pe.wait_ge(ev["acc_free"], ev_n("acc_free", layer, ACC_USES["a"]))
                for k in range(2):
                    rows(y_hi[:, k, :], y_lo[:, k, :], "ac", 11 + k, layer, it, start=first and k == 0)
                pe.wait_ge(ev["pc"], ev_n("pc", layer, it * 5 + 5))
                o = fill("S1", "oc", layer, it)
                for t in range(TOK):
                    for e in range(2):
                        use = [(n, k, g) for n, (k, ee, g) in enumerate(blocks)
                               if ee == e and (k == 0) == (t == 0)]
                        for m, (n, k, g) in enumerate(use):
                            v = val[:, 1 if k == 2 else 0, g, bass.ds(it * P + e * C_DIM, C_DIM)]
                            c = t * P + e * C_DIM
                            i = mm(o[:, c:c + C_DIM], pc[:, n, :], v, start=m == 0, stop=m == len(use) - 1)
                i.then_inc(full["S1"], 1)
                for k in range(2, 4):
                    rows(y_hi[:, k, :], y_lo[:, k, :], "ac", 11 + k, layer, it)
                pe.wait_ge(ev["nc_"], ev_n("nc_", layer, it + 1))
                o = fill("S0", "ocT", layer, it)
                for t in range(TOK):
                    i = pe.transpose(o[:, t * P:(t + 1) * P], oc_f[:, t, :], ident[:, :])
                i.then_inc(full["S0"], 1)

            pe.sem_inc(used, SLOTS)
            pe.wait_ge(cleared, 4)
            pe.wait_ge(tbl_loaded, 32)
            pe.wait_ge(consts_loaded, 64)
            for v in range(4):
                first, n = (0, A_HEADS) if v == 0 else (A_HEADS + (v - 1) * C_HEADS, C_HEADS)
                mm(acc[v // 2][v % 2][0:n, 0:ROW], tbl[:, first:first + n], oh[:, v, :], start=True, stop=True
                   ).then_inc(tables, 1)
            pe.wait_ge(tables_sb, 4)

            pe.wait_ge(x_loaded, 16)
            with pe.Fori(0, DEPTH) as layer:
                norm(0, layer)
                ffn("f1", layer)
                norm(1, layer)
                mixer_start(layer)
                acc_zero("b", layer)
                with pe.Fori(1, GROUPS) as g:
                    scan(layer, g, False)
                scan(layer, GROUPS, True)
                attention(layer, 0, first=True)
                with pe.Fori(1, AC_STEPS) as it:
                    attention(layer, it)
                for t in range(TOK):
                    for h in range(2):
                        i = mm(acc[t][h][:, :], zeros[:, 0:P], zeros[:, :], start=False, stop=True)
                i.then_inc(ev["branch_a"], 1)
                out_banks = [[fill(("W0", "W1", "S0", "S1")[2 * h + t], "branch_c", layer) for h in range(2)]
                             for t in range(TOK)]
                for k in range(4):
                    pe.wait_ge(ev["oc_lo"], ev_n("oc_lo", layer, k + 1))
                    rows(yc_hi[:, k, :], yc_lo[:, k, :], "out", k, layer, start=k == 0, stop=k == 3,
                         into=out_banks)
                turn_rows(gate_b, "mT", layer)
                pe.wait_ge(ev["acc_free"], ev_n("acc_free", layer, ACC_USES["o"]))
                for k in range(8):
                    if k % 2 == 0:
                        pe.wait_ge(ev["h_lo"], ev_n("h_lo", layer, 8 + k // 2 + 1))
                    rows(h_hi[:, k, :], h_lo[:, k, :], "out", 4 + k, layer, start=k == 0, stop=k == 7)
                norm(2, layer)
                ffn("f2", layer)
                norm(3, layer)
                pe.wait_ge(ev["cq_lo"], ev_n("cq_lo", layer, 2))
                pe.wait_ge(ev["normed"], ev_n("normed", layer, 4 * 3 + 1))
                for k in range(2):
                    rows(c_hi[:, k, :], c_lo[:, k, :], "ple", k, layer, start=k == 0, stop=k == 1)
                pe.wait_ge(ev["h_lo"], ev_n("h_lo", layer, H_AT[3] + 1))
                for k, b in enumerate(("W0", "W1", "S0", "S1")):
                    o = fill(b, "pg", layer)
                    tokens(o, "ple", 2 + 2 * k, layer, norm_r=3 if k == 0 else None)

        assert PAIRS % 2 == 1 and biggest[0] <= 8192 and TOPK == 8 * GROUPS


H_AT = (0, 4, 12, 16)


def look(seg, pos, it, layer):
    if seg == "f1pre" and pos < AHEAD:
        return tile_numbers(seg, pos, it, layer)
    reps, n = SEG_N[seg]
    if reps > 1:
        if pos >= n:
            t0 = SEG_AT[seg] + pos
            every = [t0 + n * r for r in range(reps)]
            assert len({SLOT_OF[t] for t in every}) == 1
            s, step = SLOT_OF[t0], COUNT[t0 + n] - COUNT[t0]
            assert all(COUNT[t] == COUNT[t0] + step * r for r, t in enumerate(every))
            return (layer * TILES + (it * n + t0), s, layer * USES[s] + (it * step + COUNT[t0]),
                    min(BACK[t] for t in every))
        return tile_numbers(seg, pos, it, layer)
    t0 = SEG_AT[seg] + pos
    return layer * TILES + t0, SLOT_OF[t0], layer * USES[SLOT_OF[t0]] + COUNT[t0], BACK[t0]


def _pack_layer(w, i, np_):
    w_in = w["w_in"][i]

    def feat(m, c, n=P):
        return m[:, c:c + n].reshape(KD, P, n).transpose(1, 0, 2).reshape(P, KD * n)

    def tok(m, c, n=256):
        v = feat(m, c, n)
        return [v[:, :TW], v[:, TW:]]

    def row(m, k):
        return m[k * P:(k + 1) * P, :]

    def short(m, c):
        return m[:, c:c + 512].reshape(2, P, 512).transpose(1, 0, 2).reshape(P, TW)

    def ffn(gate, up, down):
        out = []
        for j in range(PAIRS + 1):
            if j < PAIRS:
                for c in (2 * j, 2 * j + 1):
                    out += [feat(gate, c * P), feat(up, c * P)]
            if j > 0:
                out += [row(down, 2 * j - 2), row(down, 2 * j - 1)]
        return out

    tiles = ffn(w["ffn1_gate"][i], w["ffn1_up"][i], w["ffn1_down"][i])
    tiles += tok(w_in, C_CQ)
    second = np_.zeros((D_MODEL, 256), np_.float32)
    second[:, 0:200] = w_in[:, C_CKV:C_CKV + 200]
    second[:, 200:232] = w_in[:, C_DT:C_DT + 32]
    tiles += tok(second, 0)
    for g in range(CG):
        for half in range(2):
            tiles += tok(w_in, C_QKV + g * 1536 + 1024 + half * 256)
    def group(g):
        return [feat(w_in, C_XBC + g * 256), feat(w_in, C_XBC + g * 256 + P),
                feat(w_in, C_XBC + SSM + g * P), feat(w_in, C_XBC + SSM + GROUPS * STATE + g * P)
                ] + tok(w_in, C_Z + g * 256)

    for g in range(GROUPS + 1):
        if g == 0:
            tiles += group(g)[:4] + [short(w["w_iq"][i], 0)] + group(g)[4:]
            tiles += tok(w_in, C_GB) + tok(w_in, C_GB + 256)
        elif g < GROUPS:
            tiles += group(g)
        else:
            tiles += tok(w_in, C_GB + 512) + tok(w_in, C_GB + 768)
        if g > 0:
            tiles += [row(w["w_out_b"][i], 2 * g - 2), row(w["w_out_b"][i], 2 * g - 1)]
    for it in range(AC_STEPS):
        tiles += [short(w["w_uq"][i], 512 * it)]
        for g in range(CG):
            tiles += [feat(w_in, C_QKV + g * 1536 + it * P), feat(w_in, C_QKV + g * 1536 + 512 + it * P)]
        tiles += tok(w_in, C_GA + 256 * it) + tok(w_in, C_GC + 256 * it)
        tiles += [row(w["w_out_a"][i], 4 * it + k) for k in range(4)]
    tiles += [row(w["w_out_c"][i], k) for k in range(4)] + [row(w["w_o"][i], k) for k in range(8)]
    tiles += ffn(w["ffn2_gate"][i], w["ffn2_up"][i], w["ffn2_down"][i])
    tiles += [row(w["w_ple_proj"][i], k) for k in range(2)]
    for v in range(4):
        tiles += tok(w["w_ple_gate"][i], 256 * v)
    assert len(tiles) == TILES, (len(tiles), TILES)
    return tiles


def _pack_params(w, i, np_):
    prm = np_.zeros((P, NPRM), np_.float32)
    for r, name in enumerate(("ffn1_norm", "mix_norm", "ffn2_norm", "ple_norm")):
        prm[:, G_NORM + 8 * r:G_NORM + 8 * r + 8] = w[name][i].reshape(8, P).T
    prm[:, G_CQ:G_CQ + 2] = w["cq_norm"][i].reshape(2, P).T
    prm[:, G_CKV] = w["ckv_norm"][i]
    prm[:, G_EXPA:G_EXPA + 32] = w["a_log"][i][None, :]
    prm[:, G_DTB:G_DTB + 32] = w["dt_bias"][i][None, :]
    for g in range(GROUPS):
        at = G_GRP + g * GRP
        chunks = (g * 256, g * 256 + P, SSM + g * P, SSM + GROUPS * STATE + g * P)
        for c, ch in enumerate(chunks):
            prm[:, at + 4 * c:at + 4 * c + 4] = w["conv_w"][i][:, 0, ch:ch + P].T
            prm[:, at + 16 + c] = w["conv_b"][i][ch:ch + P]
        prm[:, at + 20:at + 22] = w["ssm_norm"][i][g * 256:(g + 1) * 256].reshape(2, P).T
        prm[:, at + 22:at + 26] = w["d_skip"][i][g * HG:(g + 1) * HG][None, :]
    return prm


def _shape_constants(np_):
    j, i = np_.arange(P)[:, None], np_.arange(P)[None, :]
    mask = np_.where(i <= j, 0.0, SCORE_MASK)
    const = np_.concatenate([np_.eye(P), j <= i, j > i, mask, np_.zeros((P, P)), mask],
                            axis=1).astype(np_.float32)
    one_hot = np_.zeros((4, BUCKETS + 1, ROW), np_.float32)
    half = BUCKETS // 2
    for v, (window, step) in enumerate(((SEQ, 1),) + DILATED):
        for m in range(ROW):
            d = SEQ - 1 - m
            if d < 0 or d > window or d % step:
                one_hot[v, BUCKETS, m] = MASKED
                continue
            b = d if d < half else min(BUCKETS - 1, half + int(
                math.log(d / half) / math.log(MAX_DIST / half) * (BUCKETS - half)))
            one_hot[v, b, m] = 1.0
    return const, one_hot


def kernel(**inputs):
    import numpy as _np
    import concourse.bacc as _bacc
    from concourse import mybir as _mybir
    from concourse.bass_utils import run_bass_kernel_spmd as _run

    w = {k: _np.asarray(v) for k, v in inputs.items()}
    weights = _np.empty((DEPTH * TILES, P, TW), _np.float32)
    for i in range(DEPTH):
        for n, tile in enumerate(_pack_layer(w, i, _np)):
            weights[i * TILES + n] = tile
    const, one_hot = _shape_constants(_np)
    arrays = {
        "x_in": _np.ascontiguousarray(w["x"]),
        "weights": weights,
        "params": _np.stack([_pack_params(w, i, _np) for i in range(DEPTH)]
                            + [_np.zeros((P, NPRM), _np.float32)]),
        "final_gain": _np.ascontiguousarray(w["final_norm"]),
        "ple_in": _np.ascontiguousarray(
            w["p"][:, 0].transpose(0, 2, 1).reshape(DEPTH, 2, P, SEQ).transpose(0, 2, 1, 3)
            .reshape(DEPTH, P, 2 * SEQ)),
        "rel_bias": _np.ascontiguousarray(w["rel_bias"]),
        "constants": const,
        "one_hot": one_hot,
    }
    nc = _bacc.Bacc("TRN2", target_bir_lowering=False, num_devices=1)
    f32 = _mybir.dt.float32
    args = [nc.dram_tensor(n, a.shape, f32, kind="ExternalInput").ap() for n, a in arrays.items()]
    args.append(nc.dram_tensor("out", (1, SEQ, D_MODEL), f32, kind="ExternalOutput").ap())
    trunk(nc, *args)
    r = _run(nc, [arrays], core_ids=[0])
    return r.results[0]["out"]
```
